# Optimizing a Trainium2 kernel written in Bass

```python
import math
import jax, jax.numpy as jnp
from jax import lax
import numpy as np

D_MODEL = 2048
BATCH = 1
SEQ = 256
DEPTH = 1

CHUNK = 64
D_MIX = D_MODEL
NORM_EPS = 1e-6
DSA_WIDTH = D_MIX // 2
DSA_HEAD_DIM = 128
DSA_HEADS = DSA_WIDTH // DSA_HEAD_DIM
IDX_HEADS = 16
IDX_DIM = 64
TOPK_MAX = 256
ROPE_THETA = 10000.0
RWKV_WIDTH = D_MIX - DSA_WIDTH
RWKV_HEAD_DIM = 64
RWKV_HEADS = RWKV_WIDTH // RWKV_HEAD_DIM
DECAY_LORA = 64
AICL_LORA = 64
GATE_LORA = 160
GN_EPS = 64e-5
N_GROUPS = 4
EXPERTS_PER_GROUP = 4
N_EXPERTS = N_GROUPS * EXPERTS_PER_GROUP
TOP_K_IN_GROUP = 2
D_EXPERT = 512
DSA_SPLITS = (DSA_WIDTH, DSA_WIDTH, DSA_WIDTH, IDX_HEADS * IDX_DIM, IDX_DIM, IDX_HEADS)
RWKV_SPLITS = (RWKV_WIDTH, DECAY_LORA, RWKV_WIDTH, RWKV_WIDTH, AICL_LORA, GATE_LORA)
DSA_COLS = sum(DSA_SPLITS)
RWKV_COLS = sum(RWKV_SPLITS)
IN_COLS = DSA_COLS + RWKV_COLS


def split_cols(p, sizes):
    cuts = np.cumsum(sizes)[:-1].tolist()
    return jnp.split(p, cuts, axis=-1)

def rms_norm(x, g, eps=NORM_EPS):
    xf = x.astype(jnp.float32)
    y = xf * lax.rsqrt(jnp.mean(xf * xf, axis=-1, keepdims=True) + eps)
    return (y * g.astype(jnp.float32)).astype(x.dtype)

def rope(x, pos):
    d = x.shape[-1]
    half = d // 2
    inv = ROPE_THETA ** (-jnp.arange(half, dtype=jnp.float32) * (2.0 / d))
    ang = pos.astype(jnp.float32)[:, None] * inv[None, :]
    cos = jnp.cos(ang)[None, :, None, :]
    sin = jnp.sin(ang)[None, :, None, :]
    xf = x.astype(jnp.float32)
    x1, x2 = xf[..., :half], xf[..., half:]
    out = jnp.concatenate([x1 * cos - x2 * sin, x2 * cos + x1 * sin], axis=-1)
    return out.astype(x.dtype)

def token_shift_mix(p, mu):
    prev = jnp.pad(p, ((0, 0), (1, 0), (0, 0)))[:, :-1]
    return p + (prev - p) * mu

def dsa_mixer(q, k, v, q_idx, k_idx, w_idx, q_gain, k_gain):
    B, S = q.shape[0], q.shape[1]
    f32 = jnp.float32
    pos = jnp.arange(S)
    q = rope(rms_norm(q.reshape(B, S, DSA_HEADS, DSA_HEAD_DIM), q_gain), pos)
    k = rope(rms_norm(k.reshape(B, S, DSA_HEADS, DSA_HEAD_DIM), k_gain), pos)
    v = v.reshape(B, S, DSA_HEADS, DSA_HEAD_DIM)
    q_idx = rope(q_idx.reshape(B, S, IDX_HEADS, IDX_DIM), pos)
    k_idx = rope(k_idx[:, :, None, :], pos)[:, :, 0]
    w_idx = w_idx.astype(f32) * (IDX_HEADS ** -0.5 * IDX_DIM ** -0.5)
    top_k = min(TOPK_MAX, S // 4)
    n_blocks = S // CHUNK
    key_pos = jnp.arange(S)
    scale = DSA_HEAD_DIM ** -0.5

    def block(i):
        start = i * CHUNK
        qi_idx = lax.dynamic_slice_in_dim(q_idx, start, CHUNK, axis=1)
        wi = lax.dynamic_slice_in_dim(w_idx, start, CHUNK, axis=1)
        qi = lax.dynamic_slice_in_dim(q, start, CHUNK, axis=1)
        iscore = jnp.einsum('bqhd,bsd->bqhs', qi_idx, k_idx, preferred_element_type=f32)
        iscore = jnp.einsum('bqhs,bqh->bqs', jax.nn.relu(iscore), wi)
        admissible = key_pos < start + CHUNK
        iscore = jnp.where(admissible[None, None, :], iscore, -jnp.inf)
        sel_score, sel = lax.top_k(iscore, top_k)
        valid = jnp.isfinite(sel_score)
        k_sel = jax.vmap(lambda kb, ib: kb[ib])(k, sel)
        v_sel = jax.vmap(lambda vb, ib: vb[ib])(v, sel)
        logits = jnp.einsum('bqhd,bqkhd->bhqk', qi, k_sel, preferred_element_type=f32) * scale
        logits = jnp.where(valid[:, None, :, :], logits, -jnp.inf)
        probs = jax.nn.softmax(logits, axis=-1)
        return jnp.einsum('bhqk,bqkhd->bqhd', probs.astype(v.dtype), v_sel)

    out = lax.map(block, jnp.arange(n_blocks))
    return out.transpose(1, 0, 2, 3, 4).reshape(B, S, DSA_WIDTH)

def rwkv7_mixer(r, d_w, k, v, d_a, d_g, w0, w_decay_up, a0, w_aicl_up, w_gate_lora_up,
                k_k, k_a, r_k, ln_x_w, ln_x_b, out_dtype):
    B, S = r.shape[0], r.shape[1]
    H, N = RWKV_HEADS, RWKV_HEAD_DIM
    f32 = jnp.float32
    w = -jax.nn.softplus(-(w0 + jnp.tanh(d_w) @ w_decay_up)) - 0.5
    decay = jnp.exp(-jnp.exp(w.astype(f32)))
    a = jax.nn.sigmoid((a0 + d_a @ w_aicl_up).astype(f32))
    g = (jax.nn.sigmoid(d_g) @ w_gate_lora_up).astype(f32)
    heads = lambda t: t.astype(f32).reshape(B, S, H, N)
    kk = heads(k * k_k)
    kk = kk / jnp.maximum(jnp.sqrt(jnp.sum(kk * kk, axis=-1, keepdims=True)), 1e-12)
    k = k.astype(f32) * (1.0 + (a - 1.0) * k_a.astype(f32))
    r_h, k_h, v_h, w_h, a_h = heads(r), heads(k), heads(v), heads(decay), heads(a)
    b_h = kk * a_h

    def step(state, inp):
        r_t, w_t, k_t, v_t, kk_t, b_t = inp
        sa = jnp.einsum('bhvk,bhk->bhv', state, -kk_t)
        state = (state * w_t[:, :, None, :] + sa[..., None] * b_t[:, :, None, :]
                 + v_t[..., None] * k_t[:, :, None, :])
        return state, jnp.einsum('bhvk,bhk->bhv', state, r_t)

    xs = tuple(t.transpose(1, 0, 2, 3) for t in (r_h, w_h, k_h, v_h, kk, b_h))
    _, ys = lax.scan(step, jnp.zeros((B, H, N, N), f32), xs)
    y = ys.transpose(1, 0, 2, 3)
    mu = jnp.mean(y, axis=-1, keepdims=True)
    var = jnp.mean(jnp.square(y - mu), axis=-1, keepdims=True)
    y = ((y - mu) * lax.rsqrt(var + GN_EPS)).reshape(B, S, RWKV_WIDTH)
    y = y * ln_x_w.astype(f32) + ln_x_b.astype(f32)
    bonus = jnp.sum(r_h * k_h * r_k.astype(f32), axis=-1, keepdims=True) * v_h
    y = (y + bonus.reshape(B, S, RWKV_WIDTH)) * g
    return y.astype(out_dtype)

def hier_moe(h, w_route_group, b_route_group, w_route_expert, b_route_expert,
             w_e_gate, w_e_up, w_e_down):
    B, S, D = h.shape
    f32 = jnp.float32
    t = h.reshape(B * S, D)
    grp_prob = jax.nn.softmax((t @ w_route_group).astype(f32) + b_route_group.astype(f32), axis=-1)
    p_grp, g_sel = lax.top_k(grp_prob, 1)
    exp_logits = ((t @ w_route_expert).astype(f32) + b_route_expert.astype(f32))
    exp_logits = exp_logits.reshape(-1, N_GROUPS, EXPERTS_PER_GROUP)
    exp_logits = jnp.take_along_axis(exp_logits, g_sel[:, :, None], axis=1)[:, 0]
    p_exp, e_sel = lax.top_k(jax.nn.softmax(exp_logits, axis=-1), TOP_K_IN_GROUP)
    p_exp = p_exp / jnp.sum(p_exp, axis=-1, keepdims=True)
    gate_w = p_grp * p_exp
    expert_id = g_sel * EXPERTS_PER_GROUP + e_sel
    combine = jnp.sum(jax.nn.one_hot(expert_id, N_EXPERTS, dtype=f32) * gate_w[..., None], axis=1)
    y = jnp.zeros((B * S, D), f32)
    for e in range(N_EXPERTS):
        he = jax.nn.silu(t @ w_e_gate[e]) * (t @ w_e_up[e])
        y = y + combine[:, e:e + 1] * (he @ w_e_down[e]).astype(f32)
    return y.reshape(B, S, D).astype(h.dtype)

def first_inputs(seed: int = 0) -> dict:
    key = jax.random.key(seed)
    ks = jax.random.split(key, 32)
    f32 = jnp.float32
    nrm = lambda k, shape, s: jax.random.normal(k, shape, f32) * s
    L, D = DEPTH, D_MODEL
    return {
        'x': jax.random.normal(ks[0], (BATCH, SEQ, D), f32),
        'g_mix': 1.0 + nrm(ks[1], (L, D), 0.02),
        'w_in': nrm(ks[2], (L, D, IN_COLS), D ** -0.5),
        'rwkv_shift_mix': jax.random.uniform(ks[3], (L, RWKV_COLS), f32),
        'q_gain': 1.0 + nrm(ks[4], (L, DSA_HEAD_DIM), 0.02),
        'k_gain': 1.0 + nrm(ks[5], (L, DSA_HEAD_DIM), 0.02),
        'w0': jax.random.uniform(ks[6], (L, RWKV_WIDTH), f32, -6.0, -1.0),
        'w_decay_up': nrm(ks[7], (L, DECAY_LORA, RWKV_WIDTH), 0.1),
        'a0': nrm(ks[8], (L, RWKV_WIDTH), 0.1),
        'w_aicl_up': nrm(ks[9], (L, AICL_LORA, RWKV_WIDTH), 0.5 * AICL_LORA ** -0.5),
        'w_gate_lora_up': nrm(ks[10], (L, GATE_LORA, RWKV_WIDTH), GATE_LORA ** -0.5),
        'k_k': 0.85 + nrm(ks[11], (L, RWKV_WIDTH), 0.02),
        'k_a': 1.0 + nrm(ks[12], (L, RWKV_WIDTH), 0.02),
        'r_k': nrm(ks[13], (L, RWKV_HEADS, RWKV_HEAD_DIM), 0.1),
        'ln_x_w': 1.0 + nrm(ks[14], (L, RWKV_WIDTH), 0.02),
        'ln_x_b': nrm(ks[15], (L, RWKV_WIDTH), 0.01),
        'w_out': nrm(ks[16], (L, D_MIX, D), D_MIX ** -0.5),
        'g_ffn': 1.0 + nrm(ks[17], (L, D), 0.02),
        'w_route_group': nrm(ks[18], (L, D, N_GROUPS), D ** -0.5),
        'b_route_group': nrm(ks[19], (L, N_GROUPS), 0.01),
        'w_route_expert': nrm(ks[20], (L, D, N_EXPERTS), D ** -0.5),
        'b_route_expert': nrm(ks[21], (L, N_EXPERTS), 0.01),
        'w_e_gate': nrm(ks[22], (L, N_EXPERTS, D, D_EXPERT), D ** -0.5),
        'w_e_up': nrm(ks[23], (L, N_EXPERTS, D, D_EXPERT), D ** -0.5),
        'w_e_down': nrm(ks[24], (L, N_EXPERTS, D_EXPERT, D), D_EXPERT ** -0.5),
    }

def first_block(x, g_mix, w_in, rwkv_shift_mix, q_gain, k_gain, w0, w_decay_up, a0, w_aicl_up,
              w_gate_lora_up, k_k, k_a, r_k, ln_x_w, ln_x_b, w_out, g_ffn, w_route_group,
              b_route_group, w_route_expert, b_route_expert, w_e_gate, w_e_up, w_e_down):
    for l in range(DEPTH):
        h = rms_norm(x, g_mix[l])
        proj = h @ w_in[l]
        p_dsa, p_rwkv = proj[..., :DSA_COLS], proj[..., DSA_COLS:]
        q, k, v, q_idx, k_idx, w_idx = split_cols(p_dsa, DSA_SPLITS)
        y_dsa = dsa_mixer(q, k, v, q_idx, k_idx, w_idx, q_gain[l], k_gain[l])
        p_rwkv = token_shift_mix(p_rwkv, rwkv_shift_mix[l])
        r, d_w, kr, vr, d_a, d_g = split_cols(p_rwkv, RWKV_SPLITS)
        y_rwkv = rwkv7_mixer(r, d_w, kr, vr, d_a, d_g, w0[l], w_decay_up[l], a0[l], w_aicl_up[l],
                             w_gate_lora_up[l], k_k[l], k_a[l], r_k[l], ln_x_w[l], ln_x_b[l],
                             x.dtype)
        x = x + jnp.concatenate([y_dsa.astype(x.dtype), y_rwkv], axis=-1) @ w_out[l]
        x = x + hier_moe(rms_norm(x, g_ffn[l]), w_route_group[l], b_route_group[l],
                         w_route_expert[l], b_route_expert[l], w_e_gate[l], w_e_up[l],
                         w_e_down[l])
    return x


A_HEADS = 8
A_EXPAND = 128
A_HEAD_V = 128
A_WIDTH = A_HEADS * A_EXPAND
A_CHUNK = 16
B_GROUPS = ((128, 1), (512, 4), (2048, 16))
B_HEADS_PER_GROUP = 4
B_HEADS = B_HEADS_PER_GROUP * len(B_GROUPS)
B_HEAD_DIM = 64
B_WIDTH = B_HEADS * B_HEAD_DIM
B_OUT = B_HEADS_PER_GROUP * B_HEAD_DIM
C_WIDTH = 768
C_KERNEL = 31
REL_BUCKETS = 32
REL_MAX_DIST = 2048
D_FF = 4 * D_MODEL
N_BRANCH = 3
IN_SPLITS = (A_WIDTH, A_WIDTH, A_HEADS * A_HEAD_V, A_HEADS * A_HEAD_V,
             B_WIDTH, B_WIDTH, B_WIDTH, C_WIDTH, C_WIDTH)
IN_WIDTH = sum(IN_SPLITS)
EPS = 1e-6
MASK_VALUE = -1e30
TINY = 1e-30


def rms_norm_2(x, w):
    xf = x.astype(jnp.float32)
    y = xf * lax.rsqrt(jnp.mean(xf * xf, axis=-1, keepdims=True) + EPS)
    return (y * w).astype(x.dtype)

def layer_norm(x, g, b):
    xf = x.astype(jnp.float32)
    mu = jnp.mean(xf, axis=-1, keepdims=True)
    var = jnp.mean(jnp.square(xf - mu), axis=-1, keepdims=True)
    return ((xf - mu) * lax.rsqrt(var + EPS) * g + b).astype(x.dtype)

def split_cols_2(a, sizes):
    idx = [int(v) for v in np.cumsum(sizes)[:-1]]
    return jnp.split(a, idx, axis=-1)

def hgrn2_mixer(q_pre, f_pre, inp, og, lb, norm_w):
    f32 = jnp.float32
    Bsz, S, _ = q_pre.shape
    H, K, V, C = A_HEADS, A_EXPAND, A_HEAD_V, A_CHUNK
    N = S // C

    def chunks(a, d):
        return a.astype(f32).reshape(Bsz, N, C, H, d).transpose(0, 3, 1, 2, 4)

    lb = jnp.maximum(lb.astype(f32), 0.0).reshape(H, K)[None, :, None, None, :]
    z = chunks(f_pre, K)
    log_f = jnp.logaddexp(jnp.log(lb + TINY), jnp.log1p(-lb) + jax.nn.log_sigmoid(z))
    k = (1.0 - lb) * jax.nn.sigmoid(-z)
    q = jax.nn.silu(chunks(q_pre, K))
    v = chunks(inp, V)
    b = jnp.cumsum(log_f, axis=3)
    causal = jnp.tril(jnp.ones((C, C), bool))
    decay = jnp.exp(jnp.where(causal[:, :, None],
                              b[..., :, None, :] - b[..., None, :, :], MASK_VALUE))
    attn = jnp.einsum('bhntk,bhntsk,bhnsk->bhnts', q, decay, k)
    o = jnp.einsum('bhnts,bhnsv->bhntv', attn, v)
    b_last = b[..., -1, :]
    delta = jnp.einsum('bhnck,bhncv->bhnkv', k * jnp.exp(b_last[..., None, :] - b), v)

    def step(state, xs):
        dec, dlt = xs
        return dec[..., None] * state + dlt, state

    _, s_prev = lax.scan(step, jnp.zeros((Bsz, H, K, V), f32),
                         (jnp.moveaxis(jnp.exp(b_last), 2, 0), jnp.moveaxis(delta, 2, 0)))
    s_prev = jnp.moveaxis(s_prev, 0, 2)
    o = o + jnp.einsum('bhnck,bhnkv->bhncv', q * jnp.exp(b), s_prev)
    o = o.transpose(0, 2, 3, 1, 4).reshape(Bsz, S, H, V)
    o = rms_norm_2(o, norm_w) * jax.nn.silu(og.astype(f32).reshape(Bsz, S, H, V))
    return o.reshape(Bsz, S, H * V).astype(q_pre.dtype)

def t5_bucket(dist):
    exact = REL_BUCKETS // 2
    d = jnp.maximum(dist, 1).astype(jnp.float32)
    large = exact + (jnp.log(d / exact) / math.log(REL_MAX_DIST / exact)
                     * (REL_BUCKETS - exact)).astype(jnp.int32)
    return jnp.where(dist < exact, dist, jnp.clip(large, exact, REL_BUCKETS - 1))

def dilated_window_group(q, k, v, bias_tab, window, dil):
    f32 = jnp.float32
    Bsz, S, H, Dh = q.shape
    J = window // dil
    Q = J
    L = S // dil
    nb = -(-L // Q)
    Lp = nb * Q

    def strided(a):
        a = a.reshape(Bsz, L, dil, H, Dh).transpose(0, 2, 1, 3, 4)
        return jnp.pad(a, ((0, 0), (0, 0), (0, Lp - L), (0, 0), (0, 0)))

    def band(a):
        a = jnp.pad(a, ((0, 0), (0, 0), (Q, 0), (0, 0), (0, 0))).reshape(Bsz, dil, nb + 1, Q, H, Dh)
        return jnp.concatenate([a[:, :, :-1], a[:, :, 1:]], axis=3)

    qb = strided(q).reshape(Bsz, dil, nb, Q, H, Dh)
    kb, vb = band(strided(k)), band(strided(v))
    steps = jnp.arange(Q)[:, None] + Q - jnp.arange(2 * Q)[None, :]
    key_pos = jnp.arange(nb)[:, None] * Q + jnp.arange(2 * Q)[None, :] - Q
    valid = ((steps >= 0) & (steps <= J))[None] & (key_pos >= 0)[:, None, :]
    bias = bias_tab[t5_bucket(jnp.clip(steps, 0, J) * dil)].transpose(2, 0, 1)
    logits = (jnp.einsum('brnqhd,brnkhd->brnhqk', qb, kb).astype(f32) * (Dh ** -0.5)
              + bias.astype(f32))
    logits = jnp.where(valid[None, None, :, None], logits, MASK_VALUE)
    m = jnp.max(logits, axis=-1, keepdims=True)
    p = jnp.exp(logits - m)
    z = jnp.sum(p, axis=-1, keepdims=True)
    o = jnp.einsum('brnhqk,brnkhd->brnqhd', p / z, vb.astype(f32))
    lse = (m + jnp.log(z))[..., 0]
    o = o.reshape(Bsz, dil, Lp, H, Dh)[:, :, :L].transpose(0, 2, 1, 3, 4).reshape(Bsz, S, H, Dh)
    lse = (lse.transpose(0, 1, 2, 4, 3).reshape(Bsz, dil, Lp, H)[:, :, :L]
           .transpose(0, 2, 1, 3).reshape(Bsz, S, H))
    return o, lse

def dilated_attention_mixer(q, k, v, rel_bias):
    Bsz, S, _ = q.shape
    shp = (Bsz, S, B_HEADS, B_HEAD_DIM)
    q, k, v = q.reshape(shp), k.reshape(shp), v.reshape(shp)
    outs, lses = [], []
    for g, (window, dil) in enumerate(B_GROUPS):
        hs = slice(g * B_HEADS_PER_GROUP, (g + 1) * B_HEADS_PER_GROUP)
        o, lse = dilated_window_group(q[:, :, hs], k[:, :, hs], v[:, :, hs],
                                      rel_bias[:, hs], window, dil)
        outs.append(o)
        lses.append(lse)
    alpha = jax.nn.softmax(jnp.stack(lses, axis=0), axis=0)
    out = jnp.sum(alpha[..., None] * jnp.stack(outs, axis=0), axis=0)
    return out.reshape(Bsz, S, B_OUT).astype(q.dtype)

def conv_module(a, gate, conv_w, conv_b, ln_g, ln_b):
    u = a * jax.nn.sigmoid(gate)
    y = lax.conv_general_dilated(u, conv_w[:, None, :], window_strides=(1,),
                                 padding=((C_KERNEL - 1, 0),),
                                 dimension_numbers=('NWC', 'WIO', 'NWC'),
                                 feature_group_count=C_WIDTH) + conv_b
    return jax.nn.silu(layer_norm(y, ln_g, ln_b))

def second_inputs(seed: int = 0) -> dict:
    key = jax.random.key(seed)
    ks = jax.random.split(key, 26)
    f32 = jnp.float32

    def nrm(k, shape, scale):
        return jax.random.normal(k, shape, f32) * scale

    D = D_MODEL
    return {
        "x": nrm(ks[0], (BATCH, SEQ, D), 1.0),
        "c": nrm(ks[1], (BATCH, D), 1.0),
        "rel_bias": nrm(ks[2], (REL_BUCKETS, B_HEADS), 0.5),
        "hgrn_lb_logits": nrm(ks[3], (DEPTH, A_WIDTH), 1.0),
        "w_ada": nrm(ks[4], (DEPTH, D, 6 * D), 0.3 * D ** -0.5),
        "b_ada": nrm(ks[5], (DEPTH, 6 * D), 0.02),
        "mix_norm_pre": 1.0 + nrm(ks[6], (DEPTH, D), 0.05),
        "mix_norm_post": 1.0 + nrm(ks[7], (DEPTH, D), 0.05),
        "w_in": nrm(ks[8], (DEPTH, D, IN_WIDTH), D ** -0.5),
        "w_gate": nrm(ks[9], (DEPTH, D, N_BRANCH * D), D ** -0.5),
        "b_gate": nrm(ks[10], (DEPTH, N_BRANCH * D), 0.02),
        "hgrn_norm_w": 1.0 + nrm(ks[11], (DEPTH, A_HEAD_V), 0.05),
        "conv_w": nrm(ks[12], (DEPTH, C_KERNEL, C_WIDTH), C_KERNEL ** -0.5),
        "conv_b": nrm(ks[13], (DEPTH, C_WIDTH), 0.02),
        "conv_ln_g": 1.0 + nrm(ks[14], (DEPTH, C_WIDTH), 0.05),
        "conv_ln_b": nrm(ks[15], (DEPTH, C_WIDTH), 0.02),
        "w_a_out": nrm(ks[16], (DEPTH, A_HEADS * A_HEAD_V, D), (A_HEADS * A_HEAD_V) ** -0.5),
        "w_b_out": nrm(ks[17], (DEPTH, B_OUT, D), B_OUT ** -0.5),
        "w_c_out": nrm(ks[18], (DEPTH, C_WIDTH, D), C_WIDTH ** -0.5),
        "w_o": nrm(ks[19], (DEPTH, D, D), D ** -0.5),
        "mlp_norm_pre": 1.0 + nrm(ks[20], (DEPTH, D), 0.05),
        "mlp_norm_post": 1.0 + nrm(ks[21], (DEPTH, D), 0.05),
        "w_up": nrm(ks[22], (DEPTH, D, D_FF), D ** -0.5),
        "w_down": nrm(ks[23], (DEPTH, D_FF, D), D_FF ** -0.5),
    }

def second_block(x, c, rel_bias, hgrn_lb_logits, w_ada, b_ada, mix_norm_pre, mix_norm_post,
              w_in, w_gate, b_gate, hgrn_norm_w, conv_w, conv_b, conv_ln_g, conv_ln_b,
              w_a_out, w_b_out, w_c_out, w_o, mlp_norm_pre, mlp_norm_post, w_up, w_down):
    Bsz, S, D = x.shape
    sm = jax.nn.softmax(hgrn_lb_logits.astype(jnp.float32), axis=0)
    lower_bounds = jnp.cumsum(sm, axis=0) - sm[0]
    c_act = jax.nn.silu(c)
    for l in range(DEPTH):
        mod = c_act @ w_ada[l] + b_ada[l]
        sh1, sc1, g1, sh2, sc2, g2 = jnp.split(mod[:, None, :], 6, axis=-1)

        h = rms_norm_2(x, mix_norm_pre[l]) * (1.0 + sc1) + sh1
        a_q, a_f, a_i, a_g, b_q, b_k, b_v, c_a, c_g = split_cols_2(h @ w_in[l], IN_SPLITS)
        ya = hgrn2_mixer(a_q, a_f, a_i, a_g, lower_bounds[l], hgrn_norm_w[l])
        yb = dilated_attention_mixer(b_q, b_k, b_v, rel_bias)
        yc = conv_module(c_a, c_g, conv_w[l], conv_b[l], conv_ln_g[l], conv_ln_b[l])
        gates = jax.nn.sigmoid(h @ w_gate[l] + b_gate[l]).reshape(Bsz, S, N_BRANCH, D)
        merged = (gates[:, :, 0] * (ya @ w_a_out[l])
                  + gates[:, :, 1] * (yb @ w_b_out[l])
                  + gates[:, :, 2] * (yc @ w_c_out[l]))
        x = x + g1 * rms_norm_2(merged @ w_o[l], mix_norm_post[l])

        h = rms_norm_2(x, mlp_norm_pre[l]) * (1.0 + sc2) + sh2
        y = jnp.square(jax.nn.relu(h @ w_up[l])) @ w_down[l]
        x = x + g2 * rms_norm_2(y, mlp_norm_post[l])
    return x


def setup_inputs(seed=0):
    out = dict(first_inputs(seed))
    for name, value in second_inputs(seed + 1).items():
        if name != "x":
            out[name + "_2"] = value
    return out


def reference(
    x, g_mix, w_in, rwkv_shift_mix, q_gain, k_gain, w0, w_decay_up, a0, w_aicl_up,
    w_gate_lora_up, k_k, k_a, r_k, ln_x_w, ln_x_b, w_out, g_ffn, w_route_group, b_route_group,
    w_route_expert, b_route_expert, w_e_gate, w_e_up, w_e_down, c_2, rel_bias_2,
    hgrn_lb_logits_2, w_ada_2, b_ada_2, mix_norm_pre_2, mix_norm_post_2, w_in_2, w_gate_2,
    b_gate_2, hgrn_norm_w_2, conv_w_2, conv_b_2, conv_ln_g_2, conv_ln_b_2, w_a_out_2, w_b_out_2,
    w_c_out_2, w_o_2, mlp_norm_pre_2, mlp_norm_post_2, w_up_2, w_down_2,
):
    x = first_block(
        x, g_mix, w_in, rwkv_shift_mix, q_gain, k_gain, w0, w_decay_up, a0, w_aicl_up,
        w_gate_lora_up, k_k, k_a, r_k, ln_x_w, ln_x_b, w_out, g_ffn, w_route_group,
        b_route_group, w_route_expert, b_route_expert, w_e_gate, w_e_up, w_e_down,
    )
    return second_block(
        x, c_2, rel_bias_2, hgrn_lb_logits_2, w_ada_2, b_ada_2, mix_norm_pre_2, mix_norm_post_2,
        w_in_2, w_gate_2, b_gate_2, hgrn_norm_w_2, conv_w_2, conv_b_2, conv_ln_g_2, conv_ln_b_2,
        w_a_out_2, w_b_out_2, w_c_out_2, w_o_2, mlp_norm_pre_2, mlp_norm_post_2, w_up_2,
        w_down_2,
    )


_drawn_inputs = setup_inputs


def setup_inputs(seed=0):
    import zlib

    import numpy as np

    out = dict(_drawn_inputs(seed))
    spreads = {}
    factors = {'q_gain': 7.277,
     'k_gain': 8.0,
     'k_k': 22.336,
     'k_a': 3.0,
     'ln_x_w': 6.824,
     'ln_x_b': 26.91,
     'b_route_group': 8.0,
     'b_route_expert': 29.315,
     'rel_bias_2': 49.662,
     'mix_norm_pre_2': 5.194,
     'mix_norm_post_2': 86.251,
     'b_gate_2': 37.926,
     'hgrn_norm_w_2': 53.989,
     'conv_b_2': 64.0,
     'conv_ln_g_2': 200.0,
     'conv_ln_b_2': 200.0,
     'mlp_norm_pre_2': 21.656,
     'mlp_norm_post_2': 88.651,
     'g_ffn': 4.797}
    for name, (base, spread) in spreads.items():
        noise = np.random.default_rng([zlib.crc32(name.encode()), seed]).standard_normal(out[name].shape)
        drawn = base * np.exp(spread * noise) if base else spread * noise
        out[name] = __import__('jax').numpy.asarray(drawn.astype(out[name].dtype))
    for name, factor in factors.items():
        out[name] = (out[name] * factor).astype(out[name].dtype)
    return out
```

```python
from contextlib import ExitStack

import numpy as np
import concourse.bass as bass
from concourse import mybir

F32 = mybir.dt.float32
F32R = mybir.dt.float32r
U32 = mybir.dt.uint32
ALU = mybir.AluOpType
ACT = mybir.ActivationFunctionType
AX = mybir.AxisListType

P = 128
D = 2048
S = 256
T = S // P
KT = D // P
RING = 8
KC = 4
NB = 512

HD, NH = 128, 8
IH, ID = 16, 64
AW = NH * HD
RH, RN = 16, 64
TOPK = 64
QCH = 64
LW, LA, LG = 64, 64, 160
DSA_COLS = 3 * AW + IH * ID + ID + IH
RW_COLS = 3 * AW + LW + LA + LG
IN1 = DSA_COLS + RW_COLS
W1 = IN1 // 24
NG, EPG = 4, 4
NE = NG * EPG
FE = 512
SLICES = 16

GH, GK = 8, 128
GW = GH * GK
BH, BD = 12, 64
BGH = 4
BW = BH * BD
CW, CK = 768, 31
CT = CW // P
IN2 = 4 * GW + 3 * BW + 2 * CW
W2 = IN2 // 16
FF = 4 * D
BUCKETS, MAXD = 32, 2048
GROUPS = ((128, 1), (512, 4), (2048, 16))
BVEC = 384
NEG = -1e30
GONE = -3e38


def shape_constants():
    i = np.arange(P)
    s, t = i[:, None], i[None, :]
    same = (s // QCH) == (t // QCH)
    c = {
        "ident": np.eye(P),
        "ones": np.ones((P, P)),
        "before": (same & (s < t)),
        "upto": (same & (s <= t)),
        "after": (same & (s > t)),
        "chunk": (i[:, None] // QCH == np.arange(2)[None, :]),
    }
    for lvl in range(1, 6):
        h = 1 << lvl
        low = (s // (2 * h) == t // (2 * h)) & (s // h > t // h)
        c[f"inv{lvl}"] = low
        c[f"invT{lvl}"] = low.T
    c["inv0"] = (s // 2 == t // 2) & (s > t)
    c["invT0"] = c["inv0"].T
    c["hg_diag"] = np.eye(P)
    for lvl in range(7):
        h = 1 << lvl
        c[f"hg{lvl}"] = (s // (2 * h) == t // (2 * h)) & (s // h < t // h)
    return {k: np.ascontiguousarray(v, dtype=np.float32) for k, v in c.items()}


def rotary(width):
    half = width // 2
    inv = np.float32(10000.0) ** (-np.arange(half, dtype=np.float32) * np.float32(2.0 / width))
    ang = (np.arange(S, dtype=np.float32)[:, None] * inv[None, :]).astype(np.float32)
    both = np.stack([np.cos(ang.astype(np.float64)), np.sin(ang.astype(np.float64))])
    return both.astype(np.float32)


def bucket_table():
    out = np.zeros((len(GROUPS), BUCKETS + 1, BVEC), np.float32)
    exact = BUCKETS // 2
    for g, (window, dil) in enumerate(GROUPS):
        for j in range(BVEC):
            d = S - 1 - j
            if d < 0 or d % dil or d > window:
                out[g, BUCKETS, j] = 1
                continue
            x = np.float32(max(d, 1))
            large = exact + int(np.float32(np.log(x / np.float32(exact))) / np.float32(np.log(MAXD / exact))
                                * np.float32(BUCKETS - exact))
            out[g, d if d < exact else min(max(large, exact), BUCKETS - 1), j] = 1
    return out


CONSTS = shape_constants()
COL = {}
_n = 0
for _k, _v in CONSTS.items():
    COL[_k] = (_n, _v.shape[1])
    _n += _v.shape[1]
NCONST = _n
MAIN = COL["inv1"][0]
INV0, HG0 = COL["inv1"][0], COL["hg_diag"][0]


def over(ap, axis, n):
    a = ap.unsqueeze(axis)
    shape = list(a.shape)
    shape[axis] = n
    return a.broadcast_to(shape)


class Steps:

    def __init__(self, engine, sem):
        self.engine, self.sem, self.n = engine, sem, 0

    def __call__(self, ins):
        self.n += 1
        ins.then_inc(self.sem, 1)
        self.engine.wait_ge(self.sem, self.n)
        return ins


class Ring:

    def __init__(self, nc, sem, buf):
        self.buf = buf
        self.full = [sem(f"slot{i}_full") for i in range(RING)]
        self.free = [sem(f"slot{i}_free") for i in range(RING)]
        self.loads = self.uses = 0

    def load(self, sp, slot, src, k, cols=NB):
        sp.wait_ge(self.free[slot], k)
        dst = self.buf[:, slot, :, 0:cols]
        sp.dma_start(dst, src).then_inc(self.full[slot], 16)

    def first(self, sp, src):
        for j in range(RING):
            ap = src(0, j)
            self.load(sp, j, ap, self.loads + 1, ap.shape[-1])
        self.loads += 1

    def rest(self, sp, src, iters, body):
        per, base = body // RING, self.loads - 1
        if iters > 1:
            with sp.Fori(0, iters - 1) as i:
                for j in range(RING, body + RING):
                    ap = src(i, j) if j < body else src(i + 1, j - body)
                    self.load(sp, j % RING, ap, i * per + (base + j // RING + 1), ap.shape[-1])
        for j in range(RING, body):
            ap = src(iters - 1, j)
            self.load(sp, j % RING, ap, base + (iters - 1) * per + j // RING + 1, ap.shape[-1])
        self.loads = base + iters * per

    def use(self, pe, j, i, body, work):
        pe.wait_ge(self.full[j % RING], i * (16 * (body // RING)) + 16 * (self.uses + j // RING + 1))
        work(self.buf[:, j % RING]).then_inc(self.free[j % RING], 1)

    def done(self, engine, j, i, body):
        engine.wait_ge(self.free[j % RING], i * (body // RING) + (self.uses + j // RING + 2))

    def used(self, iters, body):
        self.uses += iters * body // RING


class Split:

    HALF = KC // 2

    def __init__(self, stage, ring, act, body, plain=0):
        self.ring, self.act, self.body, self.nc = ring, act, body, stage.chip.nc
        self.plain, self.count = plain, body - plain
        self.w = [stage.sb(f"w_{n}", [P, 4, self.HALF, NB], F32R) for n in ("hi", "lo")]
        self.a = [stage.sb(f"a_{n}", [P, KT, S], F32R) for n in ("hi", "lo")]
        self.hi_done, self.lo_done, self.half_used, self.act_hi, self.act_lo = (
            stage.sem(n) for n in ("hi_done", "lo_done", "half_used", "act_hi", "act_lo"))

    def parts(self, k, t):
        tt = slice(t * P, (t + 1) * P)
        return self.a[0][:, k, tt], self.a[1][:, k, tt]

    def begin_scalar(self, sc, cols=lambda j: NB):
        for q in range(4):
            ks = slice(q * KC, (q + 1) * KC)
            self.nc.scalar.copy(self.a[0][:, ks], self.act[:, ks]).then_inc(self.act_hi, 1)
            if q < 2:
                self.hi(sc, q, 0, cols(q))

    def begin_vector(self, ve, cols=lambda j: NB):
        for q in range(4):
            ks = slice(q * KC, (q + 1) * KC)
            ve.wait_ge(self.act_hi, q + 1)
            self.nc.vector.tensor_tensor(self.a[1][:, ks], self.act[:, ks], self.a[0][:, ks].bitcast(F32),
                                         ALU.subtract).then_inc(self.act_lo, 1)
            if q < 2:
                self.lo(ve, q, 0, cols(q))

    def begin_tensor(self, pe):
        pe.sem_inc(self.half_used, 2)

    def chunks(self, make, engine, i, first, last, cols=lambda j: NB):
        for j in range(first, last):
            make(engine, j, i, cols(j))

    def _half(self, j, half):
        return (j % 2) * 2 + half

    def _halves(self, j, half, i):
        return i * (2 * self.count) + (2 * (j - j // self.body * self.plain) + half + 1)

    def hi(self, sc, j, i, cols=NB):
        ring = self.ring
        sc.wait_ge(ring.full[j % RING], i * (16 * (self.body // RING)) + 16 * (ring.uses + j // RING + 1))
        for half in range(2):
            if half == 0:
                sc.wait_ge(self.half_used, i * self.count + (j + 1 - j // self.body * self.plain))
            else:
                ring.done(sc, j - 2 - (self.plain if j % self.body < 2 else 0), i, self.body)
            ks = slice(half * self.HALF, (half + 1) * self.HALF)
            self.nc.scalar.copy(self.w[0][:, self._half(j, half), :, 0:cols],
                                ring.buf[:, j % RING, ks, 0:cols]).then_inc(self.hi_done, 1)

    def lo(self, ve, j, i, cols=NB):
        for half in range(2):
            ve.wait_ge(self.hi_done, self._halves(j, half, i))
            ks, q = slice(half * self.HALF, (half + 1) * self.HALF), self._half(j, half)
            self.nc.vector.tensor_tensor(self.w[1][:, q, :, 0:cols], self.ring.buf[:, j % RING, ks, 0:cols],
                                         self.w[0][:, q, :, 0:cols].bitcast(F32), ALU.subtract).then_inc(self.lo_done, 1)

    def use(self, pe, j, i, out, parts, k0, first, last, cols=NB, tiles=T):
        pe.wait_ge(self.act_lo, k0 // KC + 1)
        for half in range(2):
            pe.wait_ge(self.lo_done, self._halves(j, half, i))
            for k in range(self.HALF):
                kk = half * self.HALF + k
                w_hi, w_lo = (w[:, self._half(j, half), k, 0:cols] for w in self.w)
                for t in range(tiles):
                    a_hi, a_lo = parts(k0 + kk, t)
                    passes = [(a_hi, w_hi), (a_hi, w_lo)] + ([] if a_lo is None else [(a_lo, w_hi)])
                    for n, (a, w) in enumerate(passes):
                        mm = self.nc.tensor.matmul(out(t), a, w, start=(first and kk == n == 0),
                                                   stop=(last and kk == KC - 1 and n == len(passes) - 1))
            mm.then_inc(self.half_used if half == 0 else self.ring.free[j % RING], 1)


def weight_blocks(w, cols):
    return w.rearrange("(c k p) (b n) -> b c p k n", p=P, k=KC, n=cols)


def chunk_of(view, b, c):
    if isinstance(b, int):
        return view[b, c]
    return view[bass.ds(b, 1), c].rearrange("b p k n -> (b p) k n")


def inverse_root(nc, step, x, y, tmp, asked, rooted):
    step.engine.sem_inc(asked, 1)
    step.engine.wait_ge(rooted, 1)
    step(nc.vector.reciprocal(y, y))
    step(nc.vector.tensor_tensor(tmp, y, y, ALU.mult))
    step(nc.vector.tensor_tensor(tmp, tmp, x, ALU.mult))
    step(nc.vector.tensor_scalar(tmp, tmp, -0.5, 1.5, ALU.mult, ALU.add))
    step(nc.vector.tensor_tensor(y, y, tmp, ALU.mult))


def root(nc, x, y, asked, rooted):
    nc.scalar.wait_ge(asked, 1)
    nc.scalar.activation(y, x, ACT.Sqrt).then_inc(rooted, 1)


class Chip:

    def __init__(self, nc, ctx, dram):
        self.nc, self.dram = nc, dram
        self.psum = ctx.enter_context(nc.psum_tensor("psum", [P, 8, 512], F32))
        self.const = ctx.enter_context(nc.sbuf_tensor("const", [P, MAIN], F32))
        self.ring = Ring(nc, lambda n: ctx.enter_context(nc.semaphore(n)),
                         ctx.enter_context(nc.sbuf_tensor("ring", [P, RING, KC, NB], F32)))
        self.cols = ctx.enter_context(nc.sbuf_tensor("cols", [P, P], F32))

    def c(self, name):
        at, n = COL[name]
        return self.const[:, at:at + n]


class Stage:

    def __init__(self, chip, name):
        self.chip, self.name, self.ctx, self.sems = chip, name, ExitStack(), []

    def __enter__(self):
        return self

    def __exit__(self, *error):
        if error[0] is None:
            for sem in self.sems:
                self.chip.nc.gpsimd.sem_clear(sem)
                self.chip.nc.release_semaphore(sem)
        return self.ctx.__exit__(*error)

    def sb(self, name, shape, dt=F32):
        return self.ctx.enter_context(self.chip.nc.sbuf_tensor(f"{self.name}_{name}", shape, dt))

    def sem(self, name):
        self.sems.append(self.chip.nc.alloc_semaphore(f"{self.name}_{name}"))
        return self.sems[-1]

    def steps(self, engine, name):
        return Steps(engine, self.sem(name))


CC = {}
_n = 0
for _k, _r in (("g_mix", KT), ("g_ffn", KT), ("mix_norm_pre_2", KT), ("mlp_norm_pre_2", KT), ("c_2", KT),
               ("conv_b_2", CT), ("conv_ln_g_2", CT), ("conv_ln_b_2", CT), ("hgrn_lb_logits_2", GH)):
    CC[_k] = (_n, _r)
    _n += _r
NPAR = _n


def load_parameters(chip, first_weights):
    nc, ring, d = chip.nc, chip.ring, chip.dram
    with Stage(chip, "par") as st:
        rows, zero = st.sb("rows", [P, P]), st.sb("zero", [1, RW_COLS])
        loaded, rows_in, turned, cleared, zeroed = (
            st.sem(n) for n in ("loaded", "rows_in", "turned", "cleared", "zeroed"))
        with nc.Block() as block:
            @block.sync
            def _(sp):
                sp.dma_start(chip.const[:], d["consts"][:, 0:MAIN]).then_inc(loaded, 16)
                for name, (at, n) in CC.items():
                    src = d[name]
                    if name == "conv_b_2" or len(src.shape) == 2:
                        src = src.rearrange("a (r p) -> (a r) p", p=P)
                    sp.dma_start(rows[at:at + n, :], src).then_inc(rows_in, 16)
                ring.first(sp, first_weights)
                sp.wait_ge(cleared, 1)
                sp.dma_start(d["proj1"][0:1, DSA_COLS:IN1], zero[:]).then_inc(zeroed, 16)
                sp.wait_ge(zeroed, 16)

            @block.tensor
            def _(pe):
                for slot in range(RING):
                    pe.sem_inc(ring.free[slot], 1)
                pe.wait_ge(loaded, 16)
                pe.wait_ge(rows_in, 16 * len(CC))
                nc.tensor.transpose(chip.psum[:, 0, 0:NPAR], rows[0:NPAR, :],
                                    chip.c("ident")[0:NPAR, 0:NPAR]).then_inc(turned, 1)

            @block.vector
            def _(ve):
                nc.vector.memset(zero[:], 0.0).then_inc(cleared, 1)
                ve.wait_ge(turned, 1)
                nc.vector.tensor_copy(chip.cols[:, 0:NPAR], chip.psum[:, 0, 0:NPAR]).then_inc(cleared, 1)

            @block.scalar
            def _(sc):
                at, n = CC["c_2"]
                sc.wait_ge(cleared, 2)
                nc.scalar.activation(chip.cols[:, at:at + n], chip.psum[:, 0, at:at + n], ACT.Silu)


def normed(chip, name, x, out, gain, shift=None):
    nc = chip.nc
    with Stage(chip, name) as st:
        y, mean, scale = st.sb("y", [P, T, D]), st.sb("mean", [P, T]), st.sb("scale", [P, T])
        tmp = st.sb("tmp", [P, T])
        summed, dve, asked, rooted, scaled, turned, left, left2 = (
            st.sem(n) for n in ("summed", "dve", "asked", "rooted", "scaled", "turned", "left", "left2"))
        groups = KT // 2
        with nc.Block() as block:
            @block.scalar
            def _(sc):
                for t in range(T):
                    nc.scalar.activation(y[:, t], x[:, t], ACT.Square, accum_out=mean[:, t:t + 1]).then_inc(summed, 1)
                root(nc, mean[:], scale[:], asked, rooted)
                for g in range(0, groups, 2):
                    sc.wait_ge(turned, g + 1)
                    for k in (2 * g, 2 * g + 1):
                        ins = nc.scalar.activation(out[:, k], chip.psum[:, g % 4, k % 2 * S:(k % 2 + 1) * S],
                                                   ACT.Identity, scale=gain[:, k:k + 1],
                                                   bias=0.0 if shift is None else shift[:, k:k + 1])
                    ins.then_inc(left, 1)

            @block.vector
            def _(ve):
                step = Steps(ve, dve)
                ve.wait_ge(summed, T)
                step(nc.vector.tensor_scalar(mean[:], mean[:], 1.0 / D, 1e-6, ALU.mult, ALU.add))
                inverse_root(nc, step, mean[:], scale[:], tmp[:], asked, rooted)
                for t in range(T):
                    nc.vector.tensor_scalar(y[:, t], x[:, t], scale[:, t:t + 1], None, ALU.mult).then_inc(scaled, 1)
                for g in range(1, groups, 2):
                    ve.wait_ge(turned, g + 1)
                    for k in (2 * g, 2 * g + 1):
                        ins = nc.vector.tensor_scalar(out[:, k], chip.psum[:, g % 4, k % 2 * S:(k % 2 + 1) * S],
                                                      gain[:, k:k + 1], 0.0 if shift is None else shift[:, k:k + 1],
                                                      ALU.mult, ALU.add)
                    ins.then_inc(left2, 1)

            @block.tensor
            def _(pe):
                pe.wait_ge(scaled, T)
                for g in range(groups):
                    if g >= 4:
                        pe.wait_ge((left, left2)[g % 2], g // 2 - 1)
                    for q in range(2 * T):
                        k, t = 2 * g + q // T, q % T
                        mm = nc.tensor.transpose(chip.psum[:, g % 4, q * P:(q + 1) * P],
                                                 y[:, t, k * P:(k + 1) * P], chip.c("ident"))
                    mm.then_inc(turned, 1)


def project(chip, name, act, weights, width, dst, first_row, next_weights, modulate=False):
    nc, ring, d = chip.nc, chip.ring, chip.dram
    per, iters = 2, dst.shape[1] // width // 2
    kinds = 2 if modulate else 1
    block_ = KC * kinds
    body = block_ * per
    cols = lambda j: width if j % kinds == 0 else NB
    rows = dst[first_row:first_row + S].rearrange("(t p) (b n) -> b p t n", p=P, n=width)
    mod = d["mod"].rearrange("a (b n) -> b a n", n=NB)
    c_at = CC["c_2"][0]
    with Stage(chip, name) as st:
        out = st.sb("out", [P, per, T, width])
        split = Split(st, ring, act, body)
        copied = [st.sem(f"copied{b}") for b in range(per)]
        stored = [st.sem(f"stored{b}") for b in range(per)]
        if modulate:
            c_split, mod_rows = st.sb("c", [P, KT, 2], F32R), st.sb("row", [2, per, NB])
            c_hi, c_lo = st.sem("c_hi"), st.sem("c_lo")
            silu_c = chip.cols[:, c_at:c_at + KT]
        with nc.Block() as block:
            @block.sync
            def _(sp):
                ring.rest(sp, weights, iters, body)
                ring.first(sp, next_weights)

            @block.tensor
            def _(pe):
                split.begin_tensor(pe)
                with pe.Fori(0, iters) as i:
                    for b in range(per):
                        pe.wait_ge(copied[b], i * kinds + kinds)
                        for c in range(KC):
                            j = b * block_ + c * kinds
                            split.use(pe, j, i, lambda t, b=b: chip.psum[:, b * T + t, 0:width],
                                      split.parts, c * KC, c == 0, c == KC - 1, width)
                            if modulate:
                                if b == c == 0:
                                    pe.wait_ge(c_lo, 1)
                                split.use(pe, j + 1, i, lambda t, b=b: chip.psum[0:2, per * T + b],
                                          lambda k, t: (c_split[:, k], None), c * KC, c == 0, c == KC - 1, tiles=1)

            @block.scalar
            def _(sc):
                for b in range(per):
                    sc.sem_inc(stored[b], 16 * kinds)
                if modulate:
                    nc.scalar.copy(c_split[:, :, 0], silu_c).then_inc(c_hi, 1)
                split.begin_scalar(sc, cols)

                def at(view, b, i, shape):
                    if isinstance(i, int):
                        return view[i * per + b]
                    return view[bass.ds(i * per + b, 1)].rearrange(shape)

                def store(b, i):
                    sc.wait_ge(copied[b], i * kinds + 2 * kinds)
                    sc.dma_start(at(rows, b, i, "b p t n -> (b p) t n"), out[:, b]).then_inc(stored[b], 16)
                    if modulate:
                        sc.dma_start(at(mod, b, i, "b a n -> (b a) n"), mod_rows[:, b]).then_inc(stored[b], 16)

                split.chunks(split.hi, sc, 0, 2, block_, cols)
                with sc.Fori(0, iters - 1) as i:
                    for b in range(per):
                        split.chunks(split.hi, sc, i, (b + 1) * block_, (b + 2) * block_, cols)
                        store(b, i)
                for b in range(per):
                    split.chunks(split.hi, sc, iters - 1, (b + 1) * block_, min((b + 2) * block_, body), cols)
                    store(b, iters - 1)
                for b in range(per):
                    sc.wait_ge(stored[b], 16 * kinds * (iters + 1))

            @block.vector
            def _(ve):
                for b in range(per):
                    ve.sem_inc(copied[b], kinds)
                if modulate:
                    ve.wait_ge(c_hi, 1)
                    nc.vector.tensor_tensor(c_split[:, :, 1], silu_c, c_split[:, :, 0].bitcast(F32),
                                            ALU.subtract).then_inc(c_lo, 1)
                split.begin_vector(ve, cols)

                def copy(b, i):
                    ring.done(ve, (b + 1) * block_ - 1, i, body)
                    ve.wait_ge(stored[b], i * (16 * kinds) + 16 * kinds)
                    nc.vector.tensor_copy(out[:, b], chip.psum[:, b * T:(b + 1) * T, 0:width]).then_inc(copied[b], 1)
                    if modulate:
                        nc.vector.tensor_copy(mod_rows[:, b], chip.psum[0:2, per * T + b]).then_inc(copied[b], 1)

                with ve.Fori(0, iters - 1) as i:
                    for b in range(per):
                        split.chunks(split.lo, ve, i, b * block_ + 2, (b + 1) * block_ + 2, cols)
                        copy(b, i)
                for b in range(per):
                    split.chunks(split.lo, ve, iters - 1, b * block_ + 2, min((b + 1) * block_ + 2, body), cols)
                    copy(b, iters - 1)
        ring.used(iters, body)


def sparse_attention(chip, mixT):
    nc, d = chip.nc, chip.dram
    proj = d["proj1"][1:1 + S]
    tok = lambda a, n: proj[:, a:a + n].rearrange("(t p) n -> p t n", p=P)
    q0, k0, v0, qi0 = 0, AW, 2 * AW, 3 * AW
    ki0, wi0 = qi0 + IH * ID, qi0 + IH * ID + ID
    with Stage(chip, "dsa") as st:
        qkT = st.sb("qkT", [P, 2, NH, S])
        v = st.sb("v", [P, T, AW])
        qiT, kiT = st.sb("qiT", [P, IH // 2, S]), st.sb("kiT", [P, S])
        w = st.sb("w", [P, T, IH])

        with ExitStack() as inner:
            sb = lambda n, s: inner.enter_context(nc.sbuf_tensor(f"dsa_{n}", s, F32))
            qk, rot = sb("qk", [P, 2, T, AW]), sb("rot", [P, 2, T, AW])
            tmp = sb("tmp", [P, T, AW])
            ki = sb("ki", [P, T, 2, ID])
            qir = sb("qir", [P, T, IH * ID])
            gain = sb("gain", [P, 2, HD])
            cs, csi = sb("cs", [P, 2, T, HD // 2]), sb("csi", [P, 2, T, ID // 2])
            ss = sb("ss", [P, 2, T, NH])
            rs, rt = sb("rs", [P, 2, T, NH]), sb("rt", [P, 2, T, NH])
            qk_in, idx_in, rows_in, v_in, dve, asked, rooted, ready, turned, left = (
                st.sem(n) for n in ("qk_in", "idx_in", "rows_in", "v_in", "dve", "asked", "rooted", "ready",
                                    "turned", "left"))
            qi = rot[:, 0]
            heads = lambda a, n: a.rearrange("p t (h c) -> p t h c", h=n)

            turns = []
            for g in range(IH // 4):
                turns.append(([(qir, t, (2 * g + j) * P) for j in range(2) for t in range(T)],
                              qiT[:, 2 * g:2 * g + 2]))
            for a in range(2):
                for g in range(NH // 2):
                    turns.append(([(rot[:, a], t, (2 * g + j) * P) for j in range(2) for t in range(T)],
                                  qkT[:, a, 2 * g:2 * g + 2]))

            with nc.Block() as block:
                @block.sync
                def _(sp):
                    sp.dma_start(qi, tok(qi0, IH * ID)).then_inc(idx_in, 16)
                    for j in range(2):
                        sp.dma_start(ki[:, :, j], tok(ki0, ID)).then_inc(idx_in, 16)
                    sp.dma_start(w[:], tok(wi0, IH)).then_inc(idx_in, 16)
                    for j in range(2):
                        sp.dma_start(csi[:, j], d["rope_idx"][j].rearrange("(t p) n -> p t n", p=P)).then_inc(idx_in, 16)
                    sp.dma_start(qk[:, 0], tok(q0, AW)).then_inc(qk_in, 16)
                    sp.dma_start(qk[:, 1], tok(k0, AW)).then_inc(qk_in, 16)
                    for j in range(2):
                        sp.dma_start(cs[:, j], d["rope_head"][j].rearrange("(t p) n -> p t n", p=P)).then_inc(rows_in, 16)
                    sp.dma_start(gain[:, 0], d["q_gain"].partition_broadcast(P).rearrange("p a n -> p (a n)")).then_inc(rows_in, 16)
                    sp.dma_start(gain[:, 1], d["k_gain"].partition_broadcast(P).rearrange("p a n -> p (a n)")).then_inc(rows_in, 16)
                    sp.dma_start(v[:], tok(v0, AW)).then_inc(v_in, 16)
                    sp.wait_ge(v_in, 16)

                @block.scalar
                def _(sc):
                    root(nc, ss[:], rs[:], asked, rooted)
                    for g, (_, dst) in enumerate(turns):
                        sc.wait_ge(turned, g + 1)
                        flat = chip.psum[:, g % 4].rearrange("p (k s) -> p k s", k=2)
                        nc.scalar.copy(dst, flat).then_inc(left, 1)
                    sc.wait_ge(turned, len(turns) + 1)
                    nc.scalar.copy(kiT[:], chip.psum[:, 4, 0:S]).then_inc(left, 1)

                @block.vector
                def _(ve):
                    step = Steps(ve, dve)

                    def rotate(dst, src, table, n, half, t1):
                        c, s = (over(table[:, j], 1, n) for j in range(2))
                        a, b = src[:, :, 0:half], src[:, :, half:2 * half]
                        step(nc.vector.tensor_tensor(dst[:, :, 0:half], a, c, ALU.mult))
                        step(nc.vector.tensor_tensor(t1, b, s, ALU.mult))
                        step(nc.vector.tensor_tensor(dst[:, :, 0:half], dst[:, :, 0:half], t1, ALU.subtract))
                        step(nc.vector.tensor_tensor(dst[:, :, half:], b, c, ALU.mult))
                        step(nc.vector.tensor_tensor(t1, a, s, ALU.mult))
                        return nc.vector.tensor_tensor(dst[:, :, half:], dst[:, :, half:], t1, ALU.add)

                    ve.wait_ge(idx_in, 16 * 6)
                    for t in range(T):
                        step(rotate(qir[:, t].rearrange("p (h c) -> p h c", h=IH),
                                    qi[:, t].rearrange("p (h c) -> p h c", h=IH), csi[:, :, t], IH, ID // 2,
                                    tmp[:, 0, 0:IH * ID // 2].rearrange("p (h c) -> p h c", h=IH)))
                        step(rotate(tmp[:, 1, t * P:t * P + 2 * ID].rearrange("p (h c) -> p h c", h=2),
                                    ki[:, t], csi[:, :, t], 2, ID // 2,
                                    tmp[:, 0, 0:ID].rearrange("p (h c) -> p h c", h=2)))
                    step(nc.vector.tensor_scalar(w[:], w[:], IH ** -0.5 * ID ** -0.5, None, ALU.mult))
                    ve.sem_inc(ready, 1)
                    ve.wait_ge(qk_in, 32)
                    for a in range(2):
                        sq = rot[:, 1]
                        step(nc.vector.tensor_tensor(sq, qk[:, a], qk[:, a], ALU.mult))
                        ins = nc.vector.tensor_reduce(ss[:, a], heads(sq, NH), AX.X, ALU.add)
                        step(ins)
                    step(nc.vector.tensor_scalar(ss[:], ss[:], 1.0 / HD, 1e-6, ALU.mult, ALU.add))
                    inverse_root(nc, step, ss[:], rs[:], rt[:], asked, rooted)
                    ve.wait_ge(rows_in, 64)
                    for a in range(2):
                        x = heads(qk[:, a], NH)
                        step(nc.vector.tensor_tensor(x, x, over(rs[:, a], 3, HD), ALU.mult))
                        for t in range(T):
                            step(nc.vector.tensor_tensor(x[:, t], x[:, t], over(gain[:, a], 1, NH), ALU.mult))
                            step(rotate(rot[:, a, t].rearrange("p (h c) -> p h c", h=NH), x[:, t], cs[:, :, t], NH, HD // 2,
                                        tmp[:, 0, 0:AW // 2].rearrange("p (h c) -> p h c", h=NH)))
                        ve.sem_inc(ready, 1)

                @block.tensor
                def _(pe):
                    pe.wait_ge(ready, 1)
                    for g, (src, _) in enumerate(turns):
                        if g == IH // 4:
                            pe.wait_ge(ready, 2)
                        if g == IH // 4 + NH // 2:
                            pe.wait_ge(ready, 3)
                        if g >= 4:
                            pe.wait_ge(left, g - 3)
                        for q, (x, t, at) in enumerate(src):
                            mm = nc.tensor.transpose(chip.psum[:, g % 4, q * P:(q + 1) * P], x[:, t, at:at + P],
                                                     chip.c("ident"))
                        mm.then_inc(turned, 1)
                    for t in range(T):
                        mm = nc.tensor.transpose(chip.psum[:, 4, t * P:(t + 1) * P], tmp[:, 1, t * P:(t + 1) * P],
                                                 chip.c("ident"))
                    mm.then_inc(turned, 1)

        with ExitStack() as inner:
            sb = lambda n, s: inner.enter_context(nc.sbuf_tensor(f"dsb_{n}", s, F32))
            rl = sb("rl", [P, 2, 2, S])
            acc = sb("acc", [P, T, S])
            work, barred = sb("work", [P, T, S]), sb("barred", [P, T, S])
            top = sb("top", [P, 8])
            logit = sb("logit", [P, 4, 2, S])
            most, total = sb("most", [P, 4, 2]), sb("total", [P, 4, 2])
            prob = sb("prob", [P, 4, 2, S])
            probT = sb("probT", [P, 2, 4, P])
            scored, relued, added, dve, lg, masked, expd, normd, pt, pt_left, ov, ov_left = (
                st.sem(n) for n in ("scored", "relued", "added", "dve2", "logits", "masked", "expd", "normd",
                                    "probsT", "probsT_left", "out", "out_left"))
            keys = lambda t: (t + 1) * P
            pairs = [(t, h2) for t in range(T) for h2 in range(NH // 2)]
            bank = chip.psum
            with nc.Block() as block:
                @block.tensor
                def _(pe):
                    n = 0
                    for t in range(T):
                        for h2 in range(IH // 2):
                            if n >= 2:
                                pe.wait_ge(relued, n - 1)
                            for j in range(2):
                                lo = j * ID
                                mm = nc.tensor.matmul(bank[:, 2 * (n % 2) + j, 0:keys(t)],
                                                      qiT[lo:lo + ID, h2, t * P:(t + 1) * P],
                                                      kiT[lo:lo + ID, 0:keys(t)], start=True, stop=True)
                            mm.then_inc(scored, 1)
                            n += 1

                    def logits(m):
                        t, h2 = pairs[m]
                        if m >= 2:
                            pe.wait_ge(masked, m - 1)
                        for j in range(2):
                            h = 2 * h2 + j
                            mm = nc.tensor.matmul(bank[:, 4 + m % 2, j * S:j * S + keys(t)],
                                                  qkT[:, 0, h, t * P:(t + 1) * P], qkT[:, 1, h, 0:keys(t)],
                                                  start=True, stop=True)
                        mm.then_inc(lg, 1)

                    def output(m):
                        t, h2 = pairs[m]
                        pe.wait_ge(normd, m + 1)
                        if m >= 2:
                            pe.wait_ge(pt_left, m - 1)
                        for j in range(2):
                            for kt in range(t + 1):
                                mm = nc.tensor.transpose(bank[:, 6 + m % 2, (2 * j + kt) * P:(2 * j + kt + 1) * P],
                                                         prob[:, m % 4, j, kt * P:(kt + 1) * P], chip.c("ident"))
                        mm.then_inc(pt, 1)
                        pe.wait_ge(pt_left, m + 1)
                        if m >= 2:
                            pe.wait_ge(ov_left, m - 1)
                        for j in range(2):
                            h = 2 * h2 + j
                            for kt in range(t + 1):
                                mm = nc.tensor.matmul(bank[:, m % 2, j * P:(j + 1) * P], v[:, kt, h * HD:(h + 1) * HD],
                                                      probT[:, m % 2, 2 * j + kt], start=(kt == 0), stop=(kt == t))
                        mm.then_inc(ov, 1)

                    pe.wait_ge(relued, n)
                    for m in range(len(pairs) + 2):
                        if m < len(pairs):
                            logits(m)
                        if m >= 2:
                            output(m - 2)

                @block.scalar
                def _(sc):
                    n = 0
                    for t in range(T):
                        for h2 in range(IH // 2):
                            sc.wait_ge(scored, n + 1)
                            if n >= 2:
                                sc.wait_ge(added, n - 1)
                            nc.scalar.activation(rl[:, n % 2, :, 0:keys(t)], bank[:, 2 * (n % 2):2 * (n % 2) + 2, 0:keys(t)],
                                                 ACT.Relu).then_inc(relued, 1)
                            n += 1

                    def probs(m):
                        t, _ = pairs[m]
                        sc.wait_ge(masked, m + 1)
                        if m >= 4:
                            sc.wait_ge(pt, m - 3)
                        for j in range(2):
                            nc.scalar.activation(prob[:, m % 4, j, 0:keys(t)], logit[:, m % 4, j, 0:keys(t)], ACT.Exp,
                                                 bias=most[:, m % 4, j:j + 1],
                                                 accum_out=total[:, m % 4, j:j + 1]).then_inc(expd, 1)

                    def copies(m):
                        t, h2 = pairs[m]
                        sc.wait_ge(pt, m + 1)
                        if m >= 2:
                            sc.wait_ge(ov, m - 1)
                        src = bank[:, 6 + m % 2].rearrange("p (j k n) -> p j k n", j=2, k=2)[:, :, 0:t + 1]
                        dst = probT[:, m % 2].rearrange("p (j k) n -> p j k n", j=2)[:, :, 0:t + 1]
                        nc.scalar.copy(dst, src).then_inc(pt_left, 1)
                        sc.wait_ge(ov, m + 1)
                        nc.scalar.copy(mixT[:, 2 * h2:2 * h2 + 2, t * P:(t + 1) * P],
                                       bank[:, m % 2, 0:2 * P].rearrange("p (j n) -> p j n", j=2)).then_inc(ov_left, 1)

                    for m in range(len(pairs) + 2):
                        if m < len(pairs):
                            probs(m)
                        if m >= 2:
                            copies(m - 2)

                @block.vector
                def _(ve):
                    step = Steps(ve, dve)
                    n = 0
                    step(nc.vector.memset(work[:], NEG))
                    for t in range(T):
                        for h2 in range(IH // 2):
                            ve.wait_ge(relued, n + 1)
                            for j in range(2):
                                h, x = 2 * h2 + j, rl[:, n % 2, j, 0:keys(t)]
                                a = acc[:, t, 0:keys(t)]
                                if h == 0:
                                    step(nc.vector.tensor_scalar(a, x, w[:, t, h:h + 1], None, ALU.mult))
                                elif j == 0:
                                    step(nc.vector.scalar_tensor_tensor(a, x, w[:, t, h:h + 1], a, ALU.mult, ALU.add))
                                else:
                                    nc.vector.scalar_tensor_tensor(a, x, w[:, t, h:h + 1], a, ALU.mult,
                                                                   ALU.add).then_inc(added, 1)
                                    ve.wait_ge(added, n + 1)
                            n += 1
                        for c in range(2):
                            lo, adm = c * QCH, (2 * t + c + 1) * QCH
                            step(nc.vector.tensor_copy(work[lo:lo + QCH, t, 0:adm], acc[lo:lo + QCH, t, 0:adm]))
                        for _r in range(TOPK // 8):
                            step(nc.vector.max(top[:], work[:, t, 0:keys(t)]))
                            step(nc.vector.match_replace(work[:, t, 0:keys(t)], top[:], work[:, t, 0:keys(t)], GONE))
                        step(nc.vector.tensor_scalar(barred[:, t], work[:, t], GONE / 2, NEG, ALU.is_gt, ALU.mult))

                    def mask(m):
                        t, _ = pairs[m]
                        ve.wait_ge(lg, m + 1)
                        if m >= 4:
                            ve.wait_ge(expd, 2 * (m - 3))
                        x = logit[:, m % 4, :, 0:keys(t)]
                        src = bank[:, 4 + m % 2].rearrange("p (j n) -> p j n", j=2)[:, :, 0:keys(t)]
                        step(nc.vector.scalar_tensor_tensor(x, src, HD ** -0.5, over(barred[:, t, 0:keys(t)], 1, 2),
                                                            ALU.mult, ALU.add))
                        nc.vector.tensor_reduce(most[:, m % 4], x, AX.X, ALU.max, negate=True).then_inc(masked, 1)

                    def norm(m):
                        t, _ = pairs[m]
                        ve.wait_ge(expd, 2 * (m + 1))
                        step(nc.vector.reciprocal(total[:, m % 4], total[:, m % 4]))
                        x = prob[:, m % 4, :, 0:keys(t)]
                        nc.vector.tensor_tensor(x, x, over(total[:, m % 4], 2, keys(t)), ALU.mult).then_inc(normd, 1)

                    for m in range(len(pairs) + 1):
                        if m < len(pairs):
                            mask(m)
                        if m >= 1:
                            norm(m - 1)


def row(ap):
    return ap.partition_broadcast(P).rearrange("p a n -> p (a n)")


def rwkv(chip, mixT):
    nc, d, bank = chip.nc, chip.dram, chip.psum
    R0, W0 = 0, AW
    K0, V0 = AW + LW, 2 * AW + LW
    A0, G0 = 3 * AW + LW, 3 * AW + LW + LA
    heads = lambda a: a.rearrange("p t (h c) -> p t h c", h=RH)
    with Stage(chip, "rw") as st:
        cur = st.sb("cur", [P, T, RW_COLS])
        wide = [st.sb(f"wide{i}", [P, T, AW]) for i in range(4)]
        pool_ = st.sb("pool", [P, 10080 + 240])
        bonus, norm, stat = st.sb("bonus", [P, T, RH]), st.sb("norm", [P, T, RH]), st.sb("stat", [P, T, RH])
        newton = st.sb("newton", [P, T, RH])
        lam = st.sb("lam", [P, RH // 2, 2 * T])
        logw, rate, gate, kk = wide
        r, k, v = (cur[:, :, a:a + AW] for a in (R0, K0, V0))
        prev = pool_[:, 0:T * RW_COLS].rearrange("p (t n) -> p t n", t=T)
        mu = pool_[:, T * RW_COLS:3 * RW_COLS]
        tmp = pool_[:, 0:T * AW].rearrange("p (t n) -> p t n", t=T)
        rows = pool_[:, 2048:2048 + 3 * AW].rearrange("p (j n) -> p j n", j=3)
        bias_rows = pool_[0:1, 5120:5120 + 2 * AW].rearrange("p (j n) -> p j n", j=2)
        low = pool_[:, 7168:7168 + 4 * S].rearrange("p (j s) -> p j s", j=4)

        with ExitStack() as inner:
            ups = inner.enter_context(nc.sbuf_tensor("rw_ups", [P, 2, AW], F32))
            gup2 = inner.enter_context(nc.sbuf_tensor("rw_gup2", [LG - P, AW], F32))
            gup = inner.enter_context(nc.sbuf_tensor("rw_gup", [P, AW], F32))
            cur_in, prev_in, mu_in, par_in, dve, mixed, small, turned, left, made, sig, act, cum, exps, asked, rooted = (
                st.sem(n) for n in ("cur_in", "prev_in", "mu_in", "par_in", "dve", "mixed", "small", "turned", "left",
                                    "made", "sig", "act", "cum", "exps", "asked", "rooted"))
            with nc.Block() as block:
                @block.sync
                def _(sp):
                    at = lambda r0: d["proj1"][r0:r0 + S, DSA_COLS:IN1].rearrange("(t p) n -> p t n", p=P)
                    sp.dma_start(cur[:], at(1)).then_inc(cur_in, 16)
                    sp.dma_start(prev, at(0)).then_inc(prev_in, 16)
                    sp.dma_start(mu, row(d["rwkv_shift_mix"])).then_inc(mu_in, 16)
                    sp.dma_start(ups[0:LW, 0], d["w_decay_up"][0]).then_inc(par_in, 16)
                    sp.dma_start(ups[0:LA, 1], d["w_aicl_up"][0]).then_inc(par_in, 16)
                    sp.dma_start(gup[:], d["w_gate_lora_up"][0, 0:P]).then_inc(par_in, 16)
                    sp.dma_start(gup2[:], d["w_gate_lora_up"][0, P:LG]).then_inc(par_in, 16)
                    sp.wait_ge(mixed, 1)
                    for j, name in enumerate(("k_k", "k_a", "r_k")):
                        src = d[name] if name != "r_k" else d[name].rearrange("a h c -> a (h c)")
                        sp.dma_start(rows[:, j], row(src)).then_inc(par_in, 16)
                    sp.dma_start(bias_rows[:, 0], d["w0"]).then_inc(par_in, 16)
                    sp.dma_start(bias_rows[:, 1], d["a0"]).then_inc(par_in, 16)

                @block.vector
                def _(ve):
                    step = Steps(ve, dve)
                    ve.wait_ge(cur_in, 16)
                    ve.wait_ge(prev_in, 16)
                    ve.wait_ge(mu_in, 16)
                    step(nc.vector.tensor_tensor(prev, prev, cur[:], ALU.subtract))
                    step(nc.vector.tensor_tensor(prev, prev, over(mu, 1, T), ALU.mult))
                    nc.vector.tensor_tensor(cur[:], cur[:], prev, ALU.add).then_inc(mixed, 1)
                    ve.wait_ge(mixed, 1)
                    ve.wait_ge(par_in, 16 * 9)
                    step(nc.vector.tensor_tensor(kk[:], k, over(rows[:, 0], 1, T), ALU.mult))
                    step(nc.vector.tensor_tensor(tmp, kk[:], kk[:], ALU.mult))
                    step(nc.vector.tensor_reduce(stat[:], heads(tmp), AX.X, ALU.add))
                    step(nc.vector.tensor_scalar(stat[:], stat[:], 1e-24, None, ALU.max))
                    for t in range(T):
                        ve.wait_ge(made, 3 * t + 3)
                        step(nc.vector.tensor_copy(gate[:, t].rearrange("p (b n) -> p b n", b=2), bank[:, 4:6]))
                        ve.sem_inc(left, 1)
                    ve.wait_ge(sig, 4)
                    step(nc.vector.tensor_scalar(logw[:], logw[:], -float(np.exp(-0.5)), None, ALU.mult))
                    ve.sem_inc(left, 1)
                    inverse_root(nc, step, stat[:], norm[:], newton[:], asked, rooted)
                    step(nc.vector.tensor_tensor(heads(kk[:]), heads(kk[:]), over(norm[:], 3, RN), ALU.mult))
                    step(nc.vector.scalar_tensor_tensor(tmp, rate[:], -1.0, over(rows[:, 1], 1, T), ALU.add, ALU.mult))
                    step(nc.vector.scalar_tensor_tensor(k, tmp, 1.0, k, ALU.add, ALU.mult))
                    step(nc.vector.tensor_tensor(tmp, r, k, ALU.mult))
                    step(nc.vector.tensor_tensor(tmp, tmp, over(rows[:, 2], 1, T), ALU.mult))
                    step(nc.vector.tensor_reduce(bonus[:], heads(tmp), AX.X, ALU.add))
                    step(nc.vector.tensor_tensor(rate[:], rate[:], kk[:], ALU.mult))
                    ve.wait_ge(cum, 1)
                    c4 = bank[:, 0:4].rearrange("p (t b) n -> p t b n", t=T)
                    two = lambda a: a.rearrange("p t (b n) -> p t b n", b=2)
                    step(nc.vector.tensor_tensor(two(tmp), c4, two(logw[:]), ALU.subtract))
                    ve.sem_inc(exps, 1)
                    ve.wait_ge(act, 1)
                    step(nc.vector.scalar_tensor_tensor(kk[:], kk[:], -1.0, tmp, ALU.mult, ALU.mult))
                    ve.sem_inc(exps, 1)
                    ve.wait_ge(act, 2)
                    step(nc.vector.tensor_tensor(r, r, tmp, ALU.mult))
                    ve.sem_inc(exps, 1)
                    ve.wait_ge(act, 3)
                    step(nc.vector.tensor_tensor(k, k, tmp, ALU.mult))
                    step(nc.vector.tensor_tensor(rate[:], rate[:], tmp, ALU.mult))

                @block.scalar
                def _(sc):
                    sc.wait_ge(mixed, 1)
                    nc.scalar.activation(cur[:, :, W0:W0 + LW], cur[:, :, W0:W0 + LW], ACT.Tanh).then_inc(small, 1)
                    nc.scalar.activation(cur[:, :, G0:G0 + LG], cur[:, :, G0:G0 + LG], ACT.Sigmoid).then_inc(small, 1)
                    sc.wait_ge(turned, 1)
                    for j, n in enumerate((LW, LA, P, LG - P)):
                        nc.scalar.copy(low[0:n, j], bank[0:n, j, 0:S]).then_inc(small, 1)
                    for t in range(T):
                        for j, dst in enumerate((logw, rate)):
                            sc.wait_ge(made, 3 * t + j + 1)
                            src = bank[:, 2 * j:2 * j + 2]
                            nc.scalar.activation(dst[:, t].rearrange("p (b n) -> p b n", b=2), src,
                                                 ACT.Sigmoid).then_inc(sig, 1)
                    root(nc, stat[:], norm[:], asked, rooted)
                    c4 = bank[:, 0:4].rearrange("p (t b) n -> p t b n", t=T)
                    tmp4 = tmp.rearrange("p t (b n) -> p t b n", b=2)
                    sc.wait_ge(exps, 1)
                    nc.scalar.activation(tmp, tmp, ACT.Exp).then_inc(act, 1)
                    nc.scalar.activation(lam[:].rearrange("p h c -> p (h c)"), bank[:, 6, 0:RH // 2 * 2 * T], ACT.Exp)
                    for j, sign in ((2, 1.0), (3, -1.0)):
                        sc.wait_ge(exps, j)
                        for t in range(T):
                            ins = nc.scalar.activation(tmp4[:, t], c4[:, t], ACT.Exp, scale=sign)
                        ins.then_inc(act, 1)

                @block.tensor
                def _(pe):
                    pe.wait_ge(small, 2)
                    for j, (at, n) in enumerate(((W0, LW), (A0, LA), (G0, P), (G0 + P, LG - P))):
                        for t in range(T):
                            mm = nc.tensor.transpose(bank[0:n, j, t * P:(t + 1) * P], cur[:, t, at:at + n],
                                                     chip.c("ident"))
                    mm.then_inc(turned, 1)
                    pe.wait_ge(small, 6)
                    pe.wait_ge(par_in, 16 * 9)
                    for t in range(T):
                        tt = slice(t * P, (t + 1) * P)
                        for j in range(2):
                            if t:
                                pe.wait_ge(sig, j + 1)
                            for b in range(2):
                                n = slice(b * 512, (b + 1) * 512)
                                nc.tensor.matmul(bank[:, 2 * j + b], chip.c("ones")[0:1, :], bias_rows[:, j, n],
                                                 start=True, stop=False)
                                mm = nc.tensor.matmul(bank[:, 2 * j + b], low[0:LW, j, tt], ups[0:LW, j, n],
                                                      start=False, stop=True)
                            mm.then_inc(made, 1)
                        if t:
                            pe.wait_ge(left, t)
                        for b in range(2):
                            n = slice(b * 512, (b + 1) * 512)
                            nc.tensor.matmul(bank[:, 4 + b], low[:, 2, tt], gup[:, n], start=True, stop=False)
                            mm = nc.tensor.matmul(bank[:, 4 + b], low[0:LG - P, 3, tt], gup2[:, n],
                                                  start=False, stop=True)
                        mm.then_inc(made, 1)
                    pe.wait_ge(left, 3)
                    for t in range(T):
                        for h in range(RH // 2):
                            nc.tensor.matmul(bank[:, 6, h * 2 * T + 2 * t:h * 2 * T + 2 * t + 2],
                                             logw[:, t, h * P:(h + 1) * P], chip.c("chunk"), start=True, stop=True)
                        for b in range(2):
                            mm = nc.tensor.matmul(bank[:, 2 * t + b], chip.c("upto"), logw[:, t, b * 512:(b + 1) * 512],
                                                  start=True, stop=True)
                    mm.then_inc(cum, 1)

        arT = pool_[:, 0:4096].rearrange("p (h j s) -> p h j s", h=RH // 2, j=2)
        bkT = pool_[:, 4096:8192].rearrange("p (j h s) -> p j h s", j=2, h=RH // 2)
        turned, left = st.sem("turned2"), st.sem("left2")
        turns = []
        for g in range(RH // 4):
            for x, dst in ((kk[:], arT[:, 2 * g:2 * g + 2, 0]), (r, arT[:, 2 * g:2 * g + 2, 1]),
                           (rate[:], bkT[:, 0, 2 * g:2 * g + 2]), (k, bkT[:, 1, 2 * g:2 * g + 2])):
                turns.append(([(x, t, (2 * g + j) * P) for j in range(2) for t in range(T)], dst))
        left2 = st.sem("left2b")
        with nc.Block() as block:
            @block.tensor
            def _(pe):
                for g, (src, _) in enumerate(turns):
                    if g >= 4:
                        pe.wait_ge((left, left2)[g % 2], g // 2 - 1)
                    for q, (x, t, at) in enumerate(src):
                        mm = nc.tensor.transpose(bank[:, g % 4, q * P:(q + 1) * P], x[:, t, at:at + P], chip.c("ident"))
                    mm.then_inc(turned, 1)

            @block.scalar
            def _(sc):
                for g in range(0, len(turns), 2):
                    sc.wait_ge(turned, g + 1)
                    nc.scalar.copy(turns[g][1], bank[:, g % 4].rearrange("p (k s) -> p k s", k=2)).then_inc(left, 1)

            @block.vector
            def _(ve):
                for g in range(1, len(turns), 2):
                    ve.wait_ge(turned, g + 1)
                    nc.vector.tensor_copy(turns[g][1], bank[:, g % 4].rearrange("p (k s) -> p k s", k=2)).then_inc(left2, 1)

        GR, M = 4, 8
        mat = lambda a: a.rearrange("p (m n) -> p m n", m=M)
        flat = lambda a: a.rearrange("p t n -> p (t n)")
        b_pair = lambda m: r[:, m // 4, (m % 4) * 2 * P:(m % 4 + 1) * 2 * P]
        k_pair = lambda m: flat(logw[:])[:, m * 2 * P:(m + 1) * 2 * P]
        N_, NT = mat(flat(kk[:])[:, 0:1024]), mat(flat(kk[:])[:, 1024:2048])
        AB, X = mat(pool_[:, 8192:9216]), mat(pool_[:, 9216:10240])
        y = st.sb("y", [P, T, AW])
        state, u0, u = st.sb("state", [P, GR, RN]), st.sb("u0", [P, GR, RN]), st.sb("u", [P, GR, RN])
        masks = st.sb("masks", [P, HG0 - INV0])
        dve, masks_in, prod, masked, xs, xs_left, ys, grown, su, su_left, yo, yo_left, sd, sd_left, seeded = (
            st.sem(n) for n in ("dve3", "masks_in", "prod", "masked", "xs", "xs_left", "ys", "grown", "su",
                                "su_left", "yo", "yo_left", "sd", "sd_left", "seeded"))
        mask = lambda n: masks[:, COL[n][0] - INV0:COL[n][0] - INV0 + P]
        LEVELS = 5
        with nc.Block() as block:
            @block.sync
            def _(sp):
                sp.dma_start(masks[:], d["consts"][:, INV0:HG0]).then_inc(masks_in, 16)

            @block.tensor
            def _(pe):
                for g in range(RH // GR):
                    if g:
                        pe.wait_ge(sd_left, 2 * T * g)
                        pe.wait_ge(yo_left, 2 * T * g)
                    for m in range(M):
                        hh, t = m // T, m % T
                        pair, lo = 2 * g + hh // 2, RN * (hh % 2)
                        n = M * g + m
                        if m >= 2:
                            pe.wait_ge(masked, n - 1)
                        tt = slice(t * P, (t + 1) * P)
                        rhs = arT[lo:lo + RN, pair, :, tt]
                        q = 4 * (m % 2)
                        nc.tensor.matmul(bank[:, q, 0:2 * P], bkT[lo:lo + RN, 0, pair, tt], rhs, start=True, stop=True)
                        nc.tensor.matmul(bank[:, q + 1, 0:2 * P], bkT[lo:lo + RN, 1, pair, tt], rhs, start=True, stop=True)
                        nc.tensor.matmul(bank[:, q + 2, 0:P], arT[lo:lo + RN, pair, 0, tt], bkT[lo:lo + RN, 0, pair, tt],
                                         start=True, stop=True).then_inc(prod, 1)
                    pe.wait_ge(seeded, g + 1)
                    for lvl in range(LEVELS):
                        n = LEVELS * g + lvl
                        if lvl:
                            pe.wait_ge(grown, n)
                        for m in range(M):
                            mm = nc.tensor.matmul(bank[:, m // 4, (m % 4) * P:(m % 4 + 1) * P],
                                                  b_pair(m)[:, 0:P], N_[:, m],
                                                  start=True, stop=True)
                        mm.then_inc(xs, 1)
                        pe.wait_ge(xs_left, n + 1)
                        for m in range(M):
                            nc.tensor.matmul(bank[:, 4 + m // 4, (m % 4) * P:(m % 4 + 1) * P], X[:, m], NT[:, m],
                                             start=True, stop=True)
                            mm = nc.tensor.matmul(bank[:, 2 + m // 4, (m % 4) * P:(m % 4 + 1) * P], NT[:, m], X[:, m],
                                                  start=True, stop=True)
                        mm.then_inc(ys, 1)
                    pe.wait_ge(grown, LEVELS * (g + 1))
                    for c in range(2 * T):
                        t, lo = c // 2, QCH * (c % 2)
                        n = 2 * T * g + c
                        span, ts = slice(lo, lo + QCH), slice(c * QCH, (c + 1) * QCH)
                        if c:
                            pe.wait_ge(sd_left, n)
                        for hh in range(GR):
                            m, hv = hh * T + t, slice((GR * g + hh) * RN, (GR * g + hh + 1) * RN)
                            o = bank[span, 0, hh * RN:(hh + 1) * RN]
                            nc.tensor.matmul(o, arT[:, 2 * g + hh // 2, 0, ts], state[:, hh], start=True, stop=False)
                            mm = nc.tensor.matmul(o, k_pair(m)[:, span], v[:, t, hv], start=False, stop=True)
                        mm.then_inc(su, 1)
                        pe.wait_ge(su_left, 2 * n + 1)
                        for hh in range(GR):
                            mm = nc.tensor.matmul(bank[span, 1, hh * RN:(hh + 1) * RN], NT[:, hh * T + t, span], u0[:, hh],
                                                  start=True, stop=True)
                        mm.then_inc(su, 1)
                        pe.wait_ge(su_left, 2 * n + 2)
                        for hh in range(GR):
                            h = GR * g + hh
                            hv = slice(h * RN, (h + 1) * RN)
                            o = bank[RN * (hh % 2):RN * (hh % 2) + RN, 3, hh * RN:(hh + 1) * RN]
                            nc.tensor.matmul(o, rate[span, t, hv], u[span, hh], start=True, stop=False)
                            mm = nc.tensor.matmul(o, k[span, t, hv], v[span, t, hv], start=False, stop=True)
                        mm.then_inc(sd, 1)
                        if n:
                            pe.wait_ge(yo_left, n)
                        for hh in range(GR):
                            m, hv = hh * T + t, slice((GR * g + hh) * RN, (GR * g + hh + 1) * RN)
                            o = bank[span, 2, hh * RN:(hh + 1) * RN]
                            nc.tensor.matmul(o, arT[:, 2 * g + hh // 2, 1, ts], state[:, hh], start=True, stop=False)
                            nc.tensor.matmul(o, b_pair(m)[:, P + lo:P + lo + QCH], u[:, hh], start=False, stop=False)
                            mm = nc.tensor.matmul(o, k_pair(m)[:, P + lo:P + lo + QCH], v[:, t, hv], start=False, stop=True)
                        mm.then_inc(yo, 1)

            @block.scalar
            def _(sc):
                for g in range(RH // GR):
                    for lvl in range(LEVELS):
                        n = LEVELS * g + lvl
                        sc.wait_ge(xs, n + 1)
                        nc.scalar.copy(X.rearrange("p (b m) n -> p b (m n)", b=2), bank[:, 0:2]).then_inc(xs_left, 1)
                    for c in range(2 * T):
                        t, span, n = c // 2, slice(QCH * (c % 2), QCH * (c % 2) + QCH), 2 * T * g + c
                        sc.wait_ge(yo, n + 1)
                        nc.scalar.copy(y[span, t, GR * g * RN:GR * (g + 1) * RN], bank[span, 2, 0:GR * RN]).then_inc(yo_left, 1)

            @block.vector
            def _(ve):
                step = Steps(ve, dve)
                ve.wait_ge(masks_in, 16)
                for g in range(RH // GR):
                    if g:
                        ve.wait_ge(yo, 2 * T * g)
                    step(nc.vector.memset(state[:], 0.0))
                    step(nc.vector.memset(u0[:], 0.0))
                    step(nc.vector.memset(u[:], 0.0))
                    for m in range(M):
                        n, q = M * g + m, 4 * (m % 2)
                        ve.wait_ge(prod, n + 1)
                        both = chip.const[:, COL["before"][0]:COL["before"][0] + 2 * P]
                        step(nc.vector.tensor_tensor(b_pair(m), bank[:, q, 0:2 * P], both, ALU.mult))
                        step(nc.vector.tensor_tensor(k_pair(m), bank[:, q + 1, 0:2 * P], both, ALU.mult))
                        step(nc.vector.tensor_tensor(AB[:, m], bank[:, q + 2, 0:P], chip.c("after"), ALU.mult))
                        ve.sem_inc(masked, 1)
                    for half in range(2):
                        ms = slice(4 * half, 4 * half + 4)
                        abt = r[:, half].rearrange("p (m j n) -> p m j n", m=4, j=2)[:, :, 0]
                        for dst, src, tri in ((N_, AB[:, ms], "inv0"), (NT, abt, "invT0")):
                            step(nc.vector.tensor_tensor(dst[:, ms], src, over(mask(tri), 1, 4), ALU.mult))
                            step(nc.vector.tensor_tensor(dst[:, ms], dst[:, ms], over(chip.c("ident"), 1, 4), ALU.add))
                    ve.sem_inc(seeded, 1)
                    for lvl in range(LEVELS):
                        n = LEVELS * g + lvl
                        ve.wait_ge(ys, n + 1)
                        for half in range(2):
                            ms = slice(4 * half, 4 * half + 4)
                            src = lambda b: bank[:, b + half].rearrange("p (m n) -> p m n", m=4)
                            for dst, b, name in ((N_, 2, f"inv{lvl + 1}"), (NT, 4, f"invT{lvl + 1}")):
                                step(nc.vector.copy_predicated(dst[:, ms], over(mask(name), 1, 4).bitcast(U32), src(b)))
                        ve.sem_inc(grown, 1)
                    for c in range(2 * T):
                        span, n = slice(QCH * (c % 2), QCH * (c % 2) + QCH), 2 * T * g + c
                        ve.wait_ge(su, 2 * n + 1)
                        nc.vector.tensor_copy(u0[span].rearrange("p h c -> p (h c)"), bank[span, 0, 0:GR * RN]).then_inc(su_left, 1)
                        ve.wait_ge(su, 2 * n + 2)
                        nc.vector.tensor_copy(u[span].rearrange("p h c -> p (h c)"), bank[span, 1, 0:GR * RN]).then_inc(su_left, 1)
                        ve.wait_ge(yo, n + 1)
                        ve.wait_ge(sd, n + 1)
                        for j in range(2):
                            rows_ = slice(RN * j, RN * j + RN)
                            s_ = state[rows_].rearrange("p (q j) c -> p q j c", j=2)[:, :, j]
                            b_ = bank[rows_, 3, 0:GR * RN].rearrange("p (q j c) -> p q j c", j=2, c=RN)[:, :, j]
                            step(nc.vector.tensor_tensor(s_, s_, b_, ALU.add))
                            step(nc.vector.tensor_tensor(s_, s_, over(lam[rows_, 2 * g:2 * g + 2, c], 2, RN), ALU.mult))
                        ve.sem_inc(sd_left, 1)

        sq = logw
        lnr = pool_[:, 8192:8192 + 2 * AW].rearrange("p (j n) -> p j n", j=2)
        rows_in, dve, asked, rooted, ready, turned, left = (
            st.sem(n) for n in ("rows_in4", "dve4", "asked4", "rooted4", "ready4", "turned4", "left4"))
        with nc.Block() as block:
            @block.sync
            def _(sp):
                sp.dma_start(lnr[:, 0], row(d["ln_x_w"])).then_inc(rows_in, 16)
                sp.dma_start(lnr[:, 1], row(d["ln_x_b"])).then_inc(rows_in, 16)

            @block.vector
            def _(ve):
                step = Steps(ve, dve)
                step(nc.vector.tensor_reduce(stat[:], heads(y[:]), AX.X, ALU.add))
                step(nc.vector.tensor_scalar(stat[:], stat[:], 1.0 / RN, None, ALU.mult))
                step(nc.vector.tensor_tensor(heads(y[:]), heads(y[:]), over(stat[:], 3, RN), ALU.subtract))
                step(nc.vector.tensor_tensor(sq[:], y[:], y[:], ALU.mult))
                step(nc.vector.tensor_reduce(stat[:], heads(sq[:]), AX.X, ALU.add))
                step(nc.vector.tensor_scalar(stat[:], stat[:], 1.0 / RN, 64e-5, ALU.mult, ALU.add))
                inverse_root(nc, step, stat[:], norm[:], newton[:], asked, rooted)
                step(nc.vector.tensor_tensor(heads(v), heads(v), over(bonus[:], 3, RN), ALU.mult))
                step(nc.vector.tensor_tensor(heads(y[:]), heads(y[:]), over(norm[:], 3, RN), ALU.mult))
                ve.wait_ge(rows_in, 32)
                step(nc.vector.tensor_tensor(y[:], y[:], over(lnr[:, 0], 1, T), ALU.mult))
                step(nc.vector.tensor_tensor(y[:], y[:], over(lnr[:, 1], 1, T), ALU.add))
                step(nc.vector.tensor_tensor(y[:], y[:], v, ALU.add))
                step(nc.vector.tensor_tensor(y[:], y[:], gate[:], ALU.mult))
                ve.sem_inc(ready, 1)

            @block.tensor
            def _(pe):
                pe.wait_ge(ready, 1)
                for g in range(4):
                    for q in range(4):
                        kt, t = 2 * g + q // T, q % T
                        mm = nc.tensor.transpose(bank[:, g, q * P:(q + 1) * P], y[:, t, kt * P:(kt + 1) * P], chip.c("ident"))
                    mm.then_inc(turned, 1)

            @block.scalar
            def _(sc):
                root(nc, stat[:], norm[:], asked, rooted)
                for g in range(4):
                    sc.wait_ge(turned, g + 1)
                    nc.scalar.copy(mixT[:, NH + 2 * g:NH + 2 * g + 2], bank[:, g].rearrange("p (k s) -> p k s", k=2)).then_inc(left, 1)


def square_product(chip, st, act, weights, next_weights, load, begin, leave):
    ring, bank = chip.ring, chip.psum
    body = KT // KC * (D // NB)
    left = st.sem("left")
    split = Split(st, ring, act, body)
    pair = lambda b: slice((b % 2) * T, (b % 2) * T + T)
    with chip.nc.Block() as block:
        @block.sync
        def _(sp):
            load(sp)
            ring.rest(sp, weights, 1, body)
            ring.first(sp, next_weights)

        @block.tensor
        def _(pe):
            split.begin_tensor(pe)
            for j in range(body):
                b, c = divmod(j, KC)
                if c == 0 and b >= 2:
                    pe.wait_ge(left, b - 1)
                split.use(pe, j, 0, lambda t, b=b: bank[:, pair(b).start + t], split.parts,
                          c * KC, c == 0, c == KC - 1)

        @block.scalar
        def _(sc):
            split.begin_scalar(sc)
            split.chunks(split.hi, sc, 0, 2, body)

        @block.vector
        def _(ve):
            split.begin_vector(ve)
            begin(ve)
            for b in range(D // NB):
                split.chunks(split.lo, ve, 0, b * KC + 2, min(b * KC + KC + 2, body))
                ring.done(ve, b * KC + KC - 1, 0, body)
                leave(slice(b * NB, (b + 1) * NB), bank[:, pair(b)]).then_inc(left, 1)
    ring.used(1, body)


def output_and_route(chip, mixT, x1, h2T, comb, weights, next_weights):
    nc, ring, d, bank = chip.nc, chip.ring, chip.dram, chip.psum
    with Stage(chip, "wout") as st:
        x_in = st.sem("x_in")

        def load_x(sp):
            sp.dma_start(x1[:], d["x"][0].rearrange("(t p) n -> p t n", p=P)).then_inc(x_in, 16)

        square_product(chip, st, mixT, weights, next_weights, load_x, lambda ve: ve.wait_ge(x_in, 16),
                       lambda n, pair: nc.vector.tensor_tensor(x1[:, :, n], x1[:, :, n], pair, ALU.add))

    normed(chip, "norm_ffn", x1, h2T, chip.cols[:, CC["g_ffn"][0]:CC["g_ffn"][0] + KT])

    with Stage(chip, "route") as st:
        w = st.sb("w", [P, KT, NG + NE])
        b = st.sb("b", [P, NG + NE])
        lg, gmax, gsum, gp = (st.sb(n, s) for n, s in (("lg", [P, T, NG + NE]), ("gmax", [P, T]), ("gsum", [P, T]),
                                                        ("gp", [P, T, NG])))
        pick, key, top = st.sb("pick", [P, T, NG]), st.sb("key", [P, 8]), st.sb("top", [P, T, 8])
        sel, ep, emax = st.sb("sel", [P, T, EPG]), st.sb("ep", [P, T, EPG]), st.sb("emax", [P, T])
        big, kept, share = st.sb("big", [P, T, 8]), st.sb("kept", [P, T, 8]), st.sb("share", [P, T])
        tmp = st.sb("tmp", [P, T, NG, EPG])
        w_in, b_in, made, dve, gone, exps = (st.sem(n) for n in ("w_in", "b_in", "made", "dve", "shifted", "exps"))
        with nc.Block() as block:
            @block.sync
            def _(sp):
                sp.dma_start(w[:, :, 0:NG], d["w_route_group"][0].rearrange("(k p) n -> p k n", p=P)).then_inc(w_in, 16)
                sp.dma_start(w[:, :, NG:], d["w_route_expert"][0].rearrange("(k p) n -> p k n", p=P)).then_inc(w_in, 16)
                sp.dma_start(b[:, 0:NG], row(d["b_route_group"])).then_inc(b_in, 16)
                sp.dma_start(b[:, NG:], row(d["b_route_expert"])).then_inc(b_in, 16)

            @block.tensor
            def _(pe):
                pe.wait_ge(w_in, 32)
                for t in range(T):
                    for k in range(KT):
                        mm = nc.tensor.matmul(bank[:, t, 0:NG + NE], h2T[:, k, t * P:(t + 1) * P], w[:, k],
                                              start=(k == 0), stop=(k == KT - 1))
                mm.then_inc(made, 1)

            @block.scalar
            def _(sc):
                sc.wait_ge(gone, 1)
                nc.scalar.activation(gp[:], gp[:], ACT.Exp).then_inc(exps, 1)
                sc.wait_ge(gone, 2)
                nc.scalar.activation(ep[:], ep[:], ACT.Exp).then_inc(exps, 1)

            @block.vector
            def _(ve):
                step = Steps(ve, dve)
                ve.wait_ge(made, 1)
                ve.wait_ge(b_in, 32)
                step(nc.vector.tensor_tensor(lg[:], bank[:, 0:T, 0:NG + NE], over(b[:], 1, T), ALU.add))
                g = lg[:, :, 0:NG]
                step(nc.vector.tensor_reduce(gmax[:], g, AX.X, ALU.max))
                step(nc.vector.tensor_tensor(gp[:], g, over(gmax[:], 2, NG), ALU.subtract))
                ve.sem_inc(gone, 1)
                step(nc.vector.memset(big[:], GONE))
                step(nc.vector.memset(kept[:], 0.0))
                step(nc.vector.tensor_copy(big[:, :, 0:NG], g))
                for t in range(T):
                    step(nc.vector.memset(key[:], GONE))
                    step(nc.vector.tensor_copy(key[:, 0:1], gmax[:, t:t + 1]))
                    step(nc.vector.match_replace(kept[:, t], key[:], big[:, t], 3e38))
                step(nc.vector.tensor_scalar(pick[:], kept[:, :, 0:NG], 1e38, None, ALU.is_gt))
                e = lg[:, :, NG:].rearrange("p t (g e) -> p t g e", g=NG)
                for t in range(T):
                    step(nc.vector.tensor_tensor(tmp[:, t], e[:, t], over(pick[:, t], 2, EPG), ALU.mult))
                    step(nc.vector.tensor_reduce(sel[:, t], tmp[:, t].rearrange("p g e -> p e g"), AX.X, ALU.add))
                step(nc.vector.tensor_reduce(emax[:], sel[:], AX.X, ALU.max))
                step(nc.vector.tensor_tensor(ep[:], sel[:], over(emax[:], 2, EPG), ALU.subtract))
                ve.sem_inc(gone, 1)
                ve.wait_ge(exps, 2)
                step(nc.vector.tensor_reduce(gsum[:], gp[:], AX.X, ALU.add))
                step(nc.vector.reciprocal(gsum[:], gsum[:]))
                step(nc.vector.memset(big[:], -1.0))
                step(nc.vector.tensor_copy(big[:, :, 0:EPG], ep[:]))
                for t in range(T):
                    step(nc.vector.max(top[:, t], big[:, t]))
                    step(nc.vector.memset(key[:], GONE))
                    step(nc.vector.tensor_copy(key[:, 0:2], top[:, t, 0:2]))
                    step(nc.vector.match_replace(kept[:, t], key[:], big[:, t], 3e38))
                step(nc.vector.tensor_scalar(sel[:], kept[:, :, 0:EPG], 1e38, None, ALU.is_gt))
                step(nc.vector.tensor_tensor(ep[:], ep[:], sel[:], ALU.mult))
                step(nc.vector.tensor_reduce(share[:], ep[:], AX.X, ALU.add))
                step(nc.vector.reciprocal(share[:], share[:]))
                step(nc.vector.tensor_tensor(share[:], share[:], gsum[:], ALU.mult))
                step(nc.vector.tensor_tensor(ep[:], ep[:], over(share[:], 2, EPG), ALU.mult))
                for t in range(T):
                    step(nc.vector.tensor_tensor(comb[:, t].rearrange("p (g e) -> p g e", g=NG), over(pick[:, t], 2, EPG),
                                                 over(ep[:, t], 1, NG), ALU.mult))


def feed_forward(chip, act, out, weights, next_weights, per, gated, comb=None):
    nc, ring, bank = chip.nc, chip.ring, chip.psum
    n_up = 8 if gated else 4
    one = n_up + KC
    body, last = one * per, SLICES - 1
    rounds, left = divmod(last, per)
    pair = lambda b: 4 if b % 2 == 0 else 6
    base = lambda e: n_up + e * one
    at = lambda i, e, step, first: i * (per * step) + (e * step + first)
    with Stage(chip, "moe" if gated else "mlp") as st:
        split = Split(st, ring, act, body)
        share = st.sb("share", [P, T, 1])
        act_, he = st.sb("act", [P, T, FE]), st.sb("he", [P, T, FE])
        heT = [st.sb(f"heT_{n}", [P, KC, S], F32R) for n in ("hi", "lo")]
        act_done, shared, he_done, turned, heT_hi, heT_lo, added = (
            st.sem(n) for n in ("act_done", "shared", "he_done", "turned", "heT_hi", "heT_lo", "added"))
        he_parts = lambda k, t: tuple(x[:, k, t * P:(t + 1) * P] for x in heT)

        def steps(engine, step):
            with engine.Fori(0, rounds) as i:
                for e in range(per):
                    step(i, e)
            for e in range(left):
                step(rounds, e)

        with nc.Block() as block:
            @block.sync
            def _(sp):
                ring.rest(sp, weights, SLICES // per, body)
                if next_weights is not None:
                    ring.first(sp, next_weights)

            @block.tensor
            def _(pe):
                def up(i, j0):
                    for j in range(n_up):
                        split.use(pe, j0 + j, i, lambda t, j=j: bank[:, 2 * (j // KC) + t], split.parts,
                                  j % KC * KC, j % KC == 0, j % KC == KC - 1)

                def down(i, e, j0):
                    pe.wait_ge(heT_lo, at(i, e, 1, 1))
                    for b in range(4):
                        if b > 0:
                            pe.wait_ge(added, at(i, e, 4, b))
                        split.use(pe, j0 + b, i, lambda t, b=b: bank[:, pair(b) + t], he_parts, 0, True, True)

                def turn_he(i, e):
                    pe.wait_ge(he_done, at(i, e, 1, 3))
                    for k in range(KC):
                        for t in range(T):
                            q = k % 2 * T + t
                            mm = nc.tensor.transpose(bank[:, 4 + k // 2, q * P:(q + 1) * P],
                                                     he[:, t, k * P:(k + 1) * P], chip.c("ident"))
                    mm.then_inc(turned, 1)

                def step(i, e):
                    up(i, base(e))
                    down(i, e, base(e) + n_up)
                    pe.wait_ge(added, at(i, e, 4, 4))
                    turn_he(i, e)

                split.begin_tensor(pe)
                up(0, 0)
                turn_he(0, -1)
                steps(pe, step)
                down(rounds, left, base(left))

            @block.scalar
            def _(sc):
                hi = lambda i, j0, first, end: split.chunks(split.hi, sc, i, j0 + first, j0 + end)

                def f(i, e, j):
                    ring.done(sc, j, i, body)
                    sc.wait_ge(he_done, at(i, e, 1, 2))
                    nc.scalar.activation(act_[:], bank[:, 0:2], ACT.Silu if gated else ACT.Relu).then_inc(act_done, 1)

                def turned_hi(i, e):
                    sc.wait_ge(turned, at(i, e, 1, 1))
                    for k in range(2):
                        ins = nc.scalar.copy(heT[0][:, 2 * k:2 * k + 2], bank[:, 4 + k].rearrange("p (k s) -> p k s", k=2))
                    ins.then_inc(heT_hi, 1)

                def step(i, e):
                    turned_hi(i, e)
                    hi(i, base(e), 2, 6)
                    f(i, e, base(e) + 3)
                    hi(i, base(e), 6, one + 2)

                split.begin_scalar(sc)
                hi(0, 0, 2, 6)
                f(0, -1, 3)
                hi(0, 0, 6, n_up + 2)
                steps(sc, step)
                turned_hi(rounds, left)
                hi(rounds, base(left), 2, KC)

            @block.vector
            def _(ve):
                lo = lambda i, j0, first, end: split.chunks(split.lo, ve, i, j0 + first, j0 + end)

                def f(i, e):
                    if gated:
                        m = i * per + (e + 1)
                        m = slice(m, m + 1) if isinstance(m, int) else bass.ds(m, 1)
                        nc.vector.tensor_copy(share[:], comb[:, :, m]).then_inc(shared, 1)
                        ve.wait_ge(shared, at(i, e, 1, 2))
                    ve.wait_ge(act_done, at(i, e, 1, 2))
                    if gated:
                        for t in range(T):
                            ins = nc.vector.scalar_tensor_tensor(he[:, t], act_[:, t], share[:, t], bank[:, 2 + t],
                                                                 ALU.mult, ALU.mult)
                    else:
                        ins = nc.vector.tensor_tensor(he[:], act_[:], act_[:], ALU.mult)
                    ins.then_inc(he_done, 1)

                def turned_lo(i, e):
                    ve.wait_ge(heT_hi, at(i, e, 1, 1))
                    for k in range(2):
                        ks = slice(2 * k, 2 * k + 2)
                        ins = nc.vector.tensor_tensor(heT[1][:, ks], bank[:, 4 + k].rearrange("p (k s) -> p k s", k=2),
                                                      heT[0][:, ks].bitcast(F32), ALU.subtract)
                    ins.then_inc(heT_lo, 1)

                def add(i, e, b, j):
                    ring.done(ve, j, i, body)
                    ve.wait_ge(added, at(i, e, 4, b + 1))
                    cols = slice(b * NB, (b + 1) * NB)
                    nc.vector.tensor_tensor(out[:, :, cols], out[:, :, cols], bank[:, pair(b):pair(b) + 2],
                                            ALU.add).then_inc(added, 1)

                def step(i, e):
                    turned_lo(i, e)
                    lo(i, base(e), 2, n_up + 2)
                    f(i, e)
                    for b in range(4):
                        lo(i, base(e), n_up + 2 + b, n_up + 3 + b)
                        add(i, e, b, base(e) + n_up + b)

                ve.sem_inc(added, 1)
                ve.sem_inc(he_done, 1)
                split.begin_vector(ve)
                lo(0, 0, 2, n_up + 2)
                f(0, -1)
                steps(ve, step)
                turned_lo(rounds, left)
                for b in range(4):
                    if b < 2:
                        lo(rounds, base(left), 2 + b, 3 + b)
                    add(rounds, left, b, base(left) + b)
        ring.used(SLICES // per, body)


def turn(nc, pe, bank, ident, src, turned):
    for q, x in enumerate(src):
        mm = nc.tensor.transpose(bank[:, q * P:(q + 1) * P], x, ident)
    mm.then_inc(turned, 1)


def modulation_columns(chip, modc):
    nc, d = chip.nc, chip.dram
    n = 6 * KT
    with Stage(chip, "modc") as st:
        rows, lo, bias = (st.sb(x, [n, P]) for x in ("rows", "lo", "bias"))
        loaded, dve, ready, turned = (st.sem(x) for x in ("loaded", "dve", "ready", "turned"))
        with nc.Block() as block:
            @block.sync
            def _(sp):
                for a, x in enumerate((rows, lo)):
                    sp.dma_start(x[:], d["mod"][a:a + 1].rearrange("a (r p) -> (a r) p", p=P)).then_inc(loaded, 16)
                sp.dma_start(bias[:], d["b_ada_2"].rearrange("a (r p) -> (a r) p", p=P)).then_inc(loaded, 16)

            @block.vector
            def _(ve):
                step = Steps(ve, dve)
                ve.wait_ge(loaded, 48)
                step(nc.vector.tensor_tensor(rows[:], rows[:], lo[:], ALU.add))
                step(nc.vector.tensor_tensor(rows[:], rows[:], bias[:], ALU.add))
                ve.sem_inc(ready, 1)
                ve.wait_ge(turned, 1)
                step(nc.vector.tensor_copy(modc[:], chip.psum[:, 0, 0:n]))
                for part, name in ((1, "mix_norm_pre_2"), (4, "mlp_norm_pre_2")):
                    g = modc[:, part * KT:(part + 1) * KT]
                    at = CC[name][0]
                    step(nc.vector.scalar_tensor_tensor(g, g, 1.0, chip.cols[:, at:at + KT], ALU.add, ALU.mult))

            @block.tensor
            def _(pe):
                pe.wait_ge(ready, 1)
                nc.tensor.transpose(chip.psum[:, 0, 0:n], rows[:], chip.c("ident")[0:n, 0:n]).then_inc(turned, 1)


def hgrn(chip, yT):
    nc, d, bank = chip.nc, chip.dram, chip.psum
    part = lambda j: d["proj2"][:, j * GW:(j + 1) * GW].rearrange("(t p) n -> p t n", p=P)
    LEVELS = 8
    with Stage(chip, "hg") as st:
        v, og = st.sb("v", [P, T, GW]), st.sb("og", [P, T, GW])
        qT, kT, pre, suf = (st.sb(n, [P, GH, S]) for n in ("qT", "kT", "pre", "suf"))
        qh, kh = st.sb("qh", [P, GH, S]), st.sb("kh", [P, GH, S])
        at, at01 = st.sb("at", [P, GH * T, P]), st.sb("at01", [P, GH, P])
        masks = st.sb("masks", [P, NCONST - HG0])
        normw = st.sb("normw", [P, GK])
        lb, la, l1, e = (st.sb(n, [P, GH]) for n in ("lb", "la", "l1", "e"))
        stat, rs, nt = (st.sb(n, [P, T, GH]) for n in ("stat", "rs", "nt"))
        mask = lambda n: masks[:, COL[n][0] - HG0:COL[n][0] - HG0 + P]
        (qz_in, rest_in, dve, act, asked_e, silu, turned, left, ready, sent, exps, scaled, made, taken, asked, rooted,
         out_made, done, turned2, left2) = (
            st.sem(n) for n in ("qz_in", "rest_in", "dve", "act", "asked_e", "silu", "turned", "left", "ready", "sent",
                                "exps", "scaled", "made", "taken", "asked", "rooted", "out_made", "done", "turned2",
                                "left2"))
        aq = pre[:].rearrange("p g s -> p (g s)").rearrange("p (t n) -> p t n", t=T)
        af = suf[:].rearrange("p g s -> p (g s)").rearrange("p (t n) -> p t n", t=T)
        z = kh
        o = qh[:].rearrange("p g s -> p (g s)").rearrange("p (t n) -> p t n", t=T)
        sq = kh[:].rearrange("p g s -> p (g s)").rearrange("p (t n) -> p t n", t=T)
        turns = [([af[:, t, g * P:(g + 1) * P] for g in (2 * i, 2 * i + 1) for t in range(T)], z[:, 2 * i:2 * i + 2])
                 for i in range(GH // 2)]
        turns += [([aq[:, t, g * P:(g + 1) * P] for g in (2 * i, 2 * i + 1) for t in range(T)], qT[:, 2 * i:2 * i + 2])
                  for i in range(GH // 2)]

        def halves(a, h):
            b = a[:].rearrange("p g (n b) -> p (g n) b", b=2 * h)
            return b[:, :, 0:h], b[:, :, h:2 * h]

        with nc.Block() as block:
            @block.sync
            def _(sp):
                sp.dma_start(af, part(1)).then_inc(qz_in, 16)
                sp.dma_start(aq, part(0)).then_inc(qz_in, 16)
                sp.dma_start(v[:], part(2)).then_inc(rest_in, 16)
                sp.dma_start(og[:], part(3)).then_inc(rest_in, 16)
                sp.dma_start(masks[:], d["consts"][:, HG0:NCONST]).then_inc(rest_in, 16)
                sp.dma_start(normw[:], row(d["hgrn_norm_w_2"])).then_inc(rest_in, 16)

            @block.scalar
            def _(sc):
                step = Steps(sc, act)
                sc.wait_ge(qz_in, 32)
                step(nc.scalar.activation(aq, aq, ACT.Silu))
                sc.sem_inc(silu, 1)
                sc.wait_ge(rest_in, 64)
                step(nc.scalar.activation(og[:], og[:], ACT.Silu))
                for g, (_, dst) in enumerate(turns):
                    sc.wait_ge(turned, g + 1)
                    nc.scalar.copy(dst, bank[:, g % 4].rearrange("p (k s) -> p k s", k=2)).then_inc(left, 1)
                sc.wait_ge(left, len(turns))
                step(nc.scalar.activation(kT[:], z[:], ACT.Sigmoid, scale=-1.0))
                step(nc.scalar.activation(qh[:], z[:], ACT.Abs))
                step(nc.scalar.activation(qh[:], qh[:], ACT.Exp, scale=-1.0))
                sc.wait_ge(asked_e, 1)
                step(nc.scalar.activation(e[:], e[:], ACT.Exp))
                sc.sem_inc(sent, 1)
                sc.wait_ge(asked_e, 2)
                step(nc.scalar.activation(la[:], la[:], ACT.Ln, scale=2.0 ** 50))
                step(nc.scalar.activation(l1[:], l1[:], ACT.Ln))
                step(nc.scalar.activation(qh[:], qh[:], ACT.Ln))
                sc.sem_inc(sent, 1)
                sc.wait_ge(asked_e, 3)
                step(nc.scalar.activation(suf[:], qh[:], ACT.Abs))
                step(nc.scalar.activation(suf[:], suf[:], ACT.Exp, scale=-1.0))
                sc.sem_inc(sent, 1)
                sc.wait_ge(asked_e, 4)
                step(nc.scalar.activation(suf[:], suf[:], ACT.Ln))
                sc.sem_inc(sent, 1)
                for lvl in range(LEVELS):
                    h = 1 << lvl
                    sc.wait_ge(ready, lvl + 1)
                    if lvl:
                        sc.wait_ge(made, lvl + 1)
                    nc.scalar.activation(halves(qh, h)[1], halves(pre, h)[1], ACT.Exp)
                    nc.scalar.activation(halves(kh, h)[0], halves(suf, h)[0], ACT.Exp).then_inc(exps, 1)
                root(nc, stat[:], rs[:], asked, rooted)
                for g in range(GH // 2):
                    sc.wait_ge(turned2, g + 1)
                    nc.scalar.copy(yT[:, 2 * g:2 * g + 2], bank[:, g].rearrange("p (k s) -> p k s", k=2)).then_inc(left2, 1)

            @block.vector
            def _(ve):
                step = Steps(ve, dve)
                at_, n = CC["hgrn_lb_logits_2"]
                logits = chip.cols[:, at_:at_ + n]
                step(nc.vector.tensor_tensor(e[:], logits, logits, ALU.subtract))
                ve.sem_inc(asked_e, 1)
                ve.wait_ge(sent, 1)
                step(nc.vector.reciprocal(lb[:], e[:]))
                step(nc.vector.tensor_tensor(e[:], e[:], lb[:], ALU.mult))
                step(nc.vector.tensor_tensor(lb[:], e[:], e[:], ALU.subtract))
                step(nc.vector.tensor_scalar(lb[:], lb[:], 0.0, None, ALU.max))
                step(nc.vector.tensor_scalar(la[:], lb[:], 1e-30, None, ALU.add))
                step(nc.vector.tensor_scalar(e[:], lb[:], -1.0, 1.0, ALU.mult, ALU.add))
                step(nc.vector.tensor_copy(l1[:], e[:]))
                step(nc.vector.tensor_scalar(qh[:], qh[:], 1.0, None, ALU.add))
                ve.sem_inc(asked_e, 1)
                ve.wait_ge(sent, 2)
                step(nc.vector.tensor_scalar(la[:], la[:], -50.0 * float(np.log(2.0)), None, ALU.add))
                step(nc.vector.tensor_tensor(kT[:], kT[:], over(e[:], 2, S), ALU.mult))
                step(nc.vector.scalar_tensor_tensor(pre[:], z[:], 0.0, qh[:], ALU.min, ALU.subtract))
                step(nc.vector.tensor_tensor(pre[:], pre[:], over(l1[:], 2, S), ALU.add))
                step(nc.vector.tensor_tensor(qh[:], pre[:], over(la[:], 2, S), ALU.subtract))
                ve.sem_inc(asked_e, 1)
                ve.wait_ge(sent, 3)
                step(nc.vector.tensor_scalar(suf[:], suf[:], 1.0, None, ALU.add))
                ve.sem_inc(asked_e, 1)
                ve.wait_ge(sent, 4)
                step(nc.vector.tensor_tensor(pre[:], pre[:], over(la[:], 2, S), ALU.max))
                step(nc.vector.tensor_tensor(pre[:], pre[:], suf[:], ALU.add))
                step(nc.vector.memset(suf[:], 0.0))
                step(nc.vector.memset(at[:], 0.0))
                ve.sem_inc(ready, 1)
                ve.wait_ge(rest_in, 64)

                def take(n, name):
                    ve.wait_ge(made, n + 1)
                    for b in range(4):
                        step(nc.vector.copy_predicated(at[:, 4 * b:4 * b + 4], over(mask(name), 1, 4).bitcast(U32),
                                                       bank[:, 4 * (n % 2) + b].rearrange("p (m n) -> p m n", m=4)))
                    ve.sem_inc(taken, 1)

                for lvl in range(LEVELS):
                    h = 1 << lvl
                    ve.wait_ge(exps, lvl + 1)
                    step(nc.vector.tensor_tensor(halves(qh, h)[1], halves(qh, h)[1], halves(qT, h)[1], ALU.mult))
                    step(nc.vector.tensor_tensor(halves(kh, h)[0], halves(kh, h)[0], halves(kT, h)[0], ALU.mult))
                    ve.sem_inc(scaled, 1)
                    if lvl < LEVELS - 1:
                        total = pre[:].rearrange("p g (n b) -> p (g n) b", b=2 * h)
                        first, second = total[:, :, h - 1], total[:, :, 2 * h - 1]
                        lo, hi = halves(suf, h)[0], halves(pre, h)[1]
                        step(nc.vector.tensor_tensor(lo, lo, over(second, 2, h), ALU.add))
                        step(nc.vector.tensor_tensor(hi, hi, over(first, 2, h), ALU.add))
                        ve.sem_inc(ready, 1)
                    take(lvl, "hg_diag" if lvl == 0 else f"hg{lvl - 1}")
                ve.wait_ge(made, LEVELS + 1)
                step(nc.vector.tensor_copy(at01[:].rearrange("p (b g) n -> p b (g n)", b=2), bank[:, 0:2]))
                ve.sem_inc(taken, 1)
                ve.wait_ge(out_made, 1)
                step(nc.vector.tensor_copy(o.rearrange("p t (b n) -> p (t b) n", b=2), bank[:, 4:8]))
                step(nc.vector.tensor_tensor(sq, o, o, ALU.mult))
                hd = lambda a: a.rearrange("p t (g k) -> p t g k", g=GH)
                step(nc.vector.tensor_reduce(stat[:], hd(sq), AX.X, ALU.add))
                step(nc.vector.tensor_scalar(stat[:], stat[:], 1.0 / GK, 1e-6, ALU.mult, ALU.add))
                inverse_root(nc, step, stat[:], rs[:], nt[:], asked, rooted)
                step(nc.vector.tensor_tensor(hd(o), hd(o), over(rs[:], 3, GK), ALU.mult))
                for t in range(T):
                    step(nc.vector.tensor_tensor(hd(o)[:, t], hd(o)[:, t], over(normw[:], 1, GH), ALU.mult))
                step(nc.vector.tensor_tensor(o, o, og[:], ALU.mult))
                ve.sem_inc(done, 1)

            @block.tensor
            def _(pe):
                pe.wait_ge(qz_in, 32)
                for g, (src, _) in enumerate(turns):
                    if g == GH // 2:
                        pe.wait_ge(silu, 1)
                    if g >= 4:
                        pe.wait_ge(left, g - 3)
                    turn(nc, pe, bank[:, g % 4], chip.c("ident"), src, turned)
                pe.wait_ge(left, len(turns))
                pe.wait_ge(ready, 1)
                for n in range(LEVELS + 1):
                    q, k = (qT, kT) if n == 0 else (qh, kh)
                    if n:
                        pe.wait_ge(scaled, n)
                    if n >= 2:
                        pe.wait_ge(taken, n - 1)
                    for g in range(GH):
                        for t in range(T if n < LEVELS else 1):
                            m = g * T + t if n < LEVELS else g
                            ks = slice(t * P, (t + 1) * P)
                            qs = ks if n < LEVELS else slice(P, 2 * P)
                            mm = nc.tensor.matmul(bank[:, 4 * (n % 2) + m // 4, (m % 4) * P:(m % 4 + 1) * P],
                                                  k[:, g, ks], q[:, g, qs], start=True, stop=True)
                    mm.then_inc(made, 1)
                pe.wait_ge(taken, LEVELS + 1)
                for t in range(T):
                    for g in range(GH):
                        o_ = bank[:, 4 + 2 * t + g // 4, (g % 4) * P:(g % 4 + 1) * P]
                        mm = nc.tensor.matmul(o_, at[:, g * T + t], v[:, t, g * GK:(g + 1) * GK], start=True, stop=(t == 0))
                        if t:
                            mm = nc.tensor.matmul(o_, at01[:, g], v[:, 0, g * GK:(g + 1) * GK], start=False, stop=True)
                mm.then_inc(out_made, 1)
                pe.wait_ge(done, 1)
                for g in range(GH // 2):
                    turn(nc, pe, bank[:, g], chip.c("ident"),
                         [o[:, t, k * P:(k + 1) * P] for k in (2 * g, 2 * g + 1) for t in range(T)], turned2)


def dilated_attention(chip, yT):
    nc, d, bank = chip.nc, chip.dram, chip.psum
    NG3, B0 = len(GROUPS), 4 * GW
    part = lambda j: d["proj2"][:, B0 + j * BW:B0 + (j + 1) * BW].rearrange("(t p) n -> p t n", p=P)
    with Stage(chip, "da") as st:
        q, k, v = (st.sb(n, [P, T, BW]) for n in "qkv")
        qT, kT = st.sb("qT", [P, BW // P, S]), st.sb("kT", [P, BW // P, S])
        bias = [st.sb(f"bias{t}", [P, BH, (t + 1) * P]) for t in range(T)]
        keys = lambda t: (t + 1) * P
        with ExitStack() as inner:
            sb = lambda n, s: inner.enter_context(nc.sbuf_tensor(f"da_{n}", s, F32))
            tab, tabw, hot = sb("tab", [BUCKETS + 1, BH]), sb("tabw", [BUCKETS + 1, BH, P]), sb("hot", [BUCKETS + 1, NG3, BVEC])
            vec = sb("vec", [P, BH, BVEC])
            tab_in, qkv_in, dve, wide, made, vecs, stored, back, turned, left = (
                st.sem(n) for n in ("tab_in", "qkv_in", "dve", "wide", "made", "vecs", "stored", "back", "turned", "left"))
            turns = [([x[:, t, i * P:(i + 1) * P] for i in (2 * g, 2 * g + 1) for t in range(T)], dst[:, 2 * g:2 * g + 2])
                     for x, dst in ((q, qT), (k, kT)) for g in range(BW // P // 2)]
            with nc.Block() as block:
                @block.sync
                def _(sp):
                    sp.dma_start(tab[0:BUCKETS], d["rel_bias_2"]).then_inc(tab_in, 16)
                    sp.dma_start(hot[:], d["buckets"].rearrange("g b n -> b g n")).then_inc(tab_in, 16)
                    for j, x in enumerate((q, k, v)):
                        sp.dma_start(x[:], part(j)).then_inc(qkv_in, 16)
                    sp.wait_ge(vecs, BH)
                    sp.dma_start(d["bias_rows"].rearrange("h p n -> p h n"), vec[:]).then_inc(stored, 16)
                    sp.wait_ge(stored, 16)
                    rows = d["bias_rows"]
                    for t in range(T):
                        skew = bass.AP(rows.tensor, S - 1 - P * t, [[BVEC - 1, P], [P * BVEC, BH], [1, keys(t)]])
                        sp.dma_start(bias[t][:], skew).then_inc(back, 16)
                    sp.wait_ge(back, 32)

                @block.vector
                def _(ve):
                    step = Steps(ve, dve)
                    step(nc.vector.memset(tab[BUCKETS:BUCKETS + 1], NEG))
                    ve.wait_ge(tab_in, 32)
                    step(nc.vector.tensor_copy(tabw[:], over(tab[:], 2, P)))
                    ve.sem_inc(wide, 1)
                    for h in range(BH):
                        ve.wait_ge(made, h + 1)
                        nc.vector.tensor_copy(vec[:, h], bank[:, 4 + h % 4, 0:BVEC]).then_inc(vecs, 1)

                @block.scalar
                def _(sc):
                    for g, (_, dst) in enumerate(turns):
                        sc.wait_ge(turned, g + 1)
                        nc.scalar.copy(dst, bank[:, g % 4].rearrange("p (k s) -> p k s", k=2)).then_inc(left, 1)

                @block.tensor
                def _(pe):
                    pe.wait_ge(wide, 1)
                    for h in range(BH):
                        if h >= 4:
                            pe.wait_ge(vecs, h - 3)
                        nc.tensor.matmul(bank[:, 4 + h % 4, 0:BVEC], tabw[:, h], hot[:, h // BGH], start=True,
                                         stop=True).then_inc(made, 1)
                    pe.wait_ge(qkv_in, 48)
                    for g, (src, _) in enumerate(turns):
                        if g >= 4:
                            pe.wait_ge(left, g - 3)
                        turn(nc, pe, bank[:, g % 4], chip.c("ident"), src, turned)

        items = [(t, s) for t in range(T) for s in range(BGH)]
        logit, prob = st.sb("logit", [P, 3, NG3, S]), st.sb("prob", [P, 3, NG3, S])
        probT = st.sb("probT", [P, 2, NG3 * T, P])
        most, total = st.sb("most", [P, 3, 1]), st.sb("total", [P, 3, 1])
        dve, lg, masked, expd, normd, pt, pt_left, ov, ov_left = (
            st.sem(n) for n in ("dve2", "lg", "masked", "expd", "normd", "pt", "pt_left", "ov", "ov_left"))
        with nc.Block() as block:
            @block.tensor
            def _(pe):
                def logits(m):
                    t, s = items[m]
                    if m >= 1:
                        pe.wait_ge(masked, m)
                    lo = BD * (s % 2)
                    for g in range(NG3):
                        h = g * BGH + s
                        mm = nc.tensor.matmul(bank[:, g // 2, g % 2 * S:g % 2 * S + keys(t)],
                                              qT[lo:lo + BD, h // 2, t * P:(t + 1) * P], kT[lo:lo + BD, h // 2, 0:keys(t)],
                                              start=True, stop=True)
                    mm.then_inc(lg, 1)

                def output(m):
                    t, s = items[m]
                    pe.wait_ge(normd, m + 1)
                    if m >= 2:
                        pe.wait_ge(pt_left, m - 1)
                    for i in range(NG3 * (t + 1)):
                        g, kt = i // (t + 1), i % (t + 1)
                        mm = nc.tensor.transpose(bank[:, 2 + 2 * (m % 2) + i // 4, (i % 4) * P:(i % 4 + 1) * P],
                                                 prob[:, m % 3, g, kt * P:(kt + 1) * P], chip.c("ident"))
                    mm.then_inc(pt, 1)
                    pe.wait_ge(pt_left, m + 1)
                    if m >= 2:
                        pe.wait_ge(ov_left, m - 1)
                    o = bank[BD * (s % 2):BD * (s % 2) + BD, 6 + m % 2, 0:P]
                    for i in range(NG3 * (t + 1)):
                        g, kt = i // (t + 1), i % (t + 1)
                        h = g * BGH + s
                        mm = nc.tensor.matmul(o, v[:, kt, h * BD:(h + 1) * BD], probT[:, m % 2, i],
                                              start=(i == 0), stop=(i == NG3 * (t + 1) - 1))
                    mm.then_inc(ov, 1)

                for m in range(len(items) + 1):
                    if m < len(items):
                        logits(m)
                    if m >= 1:
                        output(m - 1)

            @block.scalar
            def _(sc):
                for m in range(len(items) + 1):
                    if m < len(items):
                        t, _ = items[m]
                        sc.wait_ge(masked, m + 1)
                        if m >= 3:
                            sc.wait_ge(pt, m - 2)
                        nc.scalar.activation(prob[:, m % 3, :, 0:keys(t)], logit[:, m % 3, :, 0:keys(t)], ACT.Exp,
                                             bias=most[:, m % 3], accum_out=total[:, m % 3]).then_inc(expd, 1)
                    if m >= 1:
                        n = m - 1
                        t, s = items[n]
                        sc.wait_ge(pt, n + 1)
                        if n >= 2:
                            sc.wait_ge(ov, n - 1)
                        for b in range((NG3 * (t + 1) + 3) // 4):
                            w = min(4, NG3 * (t + 1) - 4 * b)
                            ins = nc.scalar.copy(probT[:, n % 2, 4 * b:4 * b + w].rearrange("p i n -> p (i n)"),
                                                 bank[:, 2 + 2 * (n % 2) + b, 0:w * P])
                        ins.then_inc(pt_left, 1)
                        sc.wait_ge(ov, n + 1)
                        rows = slice(BD * (s % 2), BD * (s % 2) + BD)
                        nc.scalar.copy(yT[rows, GH + s // 2, t * P:(t + 1) * P], bank[rows, 6 + n % 2, 0:P]).then_inc(ov_left, 1)

            @block.vector
            def _(ve):
                step = Steps(ve, dve)
                for m in range(len(items) + 1):
                    if m < len(items):
                        t, s = items[m]
                        ve.wait_ge(lg, m + 1)
                        if m >= 3:
                            ve.wait_ge(expd, m - 2)
                        b = bias[t][:].rearrange("p (g s) n -> p g s n", g=NG3)[:, :, s]
                        step(nc.vector.scalar_tensor_tensor(
                            logit[:, m % 3, 0:2, 0:keys(t)], bank[:, 0].rearrange("p (g n) -> p g n", g=2)[:, :, 0:keys(t)],
                            BD ** -0.5, b[:, 0:2], ALU.mult, ALU.add))
                        step(nc.vector.scalar_tensor_tensor(logit[:, m % 3, 2, 0:keys(t)], bank[:, 1, 0:keys(t)],
                                                            BD ** -0.5, b[:, 2], ALU.mult, ALU.add))
                        nc.vector.tensor_reduce(most[:, m % 3], logit[:, m % 3, :, 0:keys(t)], AX.XY, ALU.max,
                                                negate=True).then_inc(masked, 1)
                    if m >= 1:
                        n = m - 1
                        t, _ = items[n]
                        ve.wait_ge(expd, n + 1)
                        step(nc.vector.reciprocal(total[:, n % 3], total[:, n % 3]))
                        x = prob[:, n % 3, :, 0:keys(t)]
                        nc.vector.tensor_scalar(x, x, total[:, n % 3], None, ALU.mult).then_inc(normd, 1)


def convolution(chip, yT):
    nc, d, bank = chip.nc, chip.dram, chip.psum
    C0 = 4 * GW + 3 * BW
    PAD = CK - 1
    col = lambda n: chip.cols[:, CC[n][0]:CC[n][0] + CT]
    out = yT[:, GH + 2:GH + 2 + CT]
    with Stage(chip, "cv") as st:
        a, g = st.sb("a", [P, T, CW]), st.sb("g", [P, T, CW])
        uT, acc, sq = st.sb("uT", [P, CT, PAD + S]), st.sb("acc", [P, CT, S]), st.sb("sq", [P, CT, S])
        taps, tapT = st.sb("taps", [CK, CW]), st.sb("tapT", [P, CT, CK])
        mean, var, rs, nt = (st.sb(n, [P, S]) for n in ("mean", "var", "rs", "nt"))
        ag_in, taps_in, dve, sig, glu, turned, left, summed, centred, asked, rooted, ready = (
            st.sem(n) for n in ("ag_in", "taps_in", "dve", "sig", "glu", "turned", "left", "summed", "centred", "asked",
                                "rooted", "ready"))
        with nc.Block() as block:
            @block.sync
            def _(sp):
                sp.dma_start(taps[:], d["conv_w_2"][0]).then_inc(taps_in, 16)
                for x, at in ((a, C0), (g, C0 + CW)):
                    sp.dma_start(x[:], d["proj2"][:, at:at + CW].rearrange("(t p) n -> p t n", p=P)).then_inc(ag_in, 16)

            @block.tensor
            def _(pe):
                pe.wait_ge(taps_in, 16)
                for c in range(CT):
                    mm = nc.tensor.transpose(bank[:, 3, c * CK:(c + 1) * CK], taps[:, c * P:(c + 1) * P],
                                             chip.c("ident")[0:CK, 0:CK])
                mm.then_inc(turned, 1)
                pe.wait_ge(glu, 1)
                for c in range(CT // 2):
                    turn(nc, pe, bank[:, c], chip.c("ident"),
                         [a[:, t, k * P:(k + 1) * P] for k in (2 * c, 2 * c + 1) for t in range(T)], turned)
                for n in range(2):
                    pe.wait_ge(centred, n + 1)
                    for c in range(CT):
                        mm = nc.tensor.matmul(bank[:, 4 + n, 0:S], chip.c("ones"), (acc, sq)[n][:, c],
                                              start=(c == 0), stop=(c == CT - 1))
                    mm.then_inc(summed, 1)

            @block.scalar
            def _(sc):
                sc.wait_ge(ag_in, 32)
                nc.scalar.activation(g[:], g[:], ACT.Sigmoid).then_inc(sig, 1)
                for c in range(CT // 2):
                    sc.wait_ge(turned, c + 2)
                    nc.scalar.copy(uT[:, 2 * c:2 * c + 2, PAD:], bank[:, c].rearrange("p (k s) -> p k s", k=2)).then_inc(left, 1)
                root(nc, var[:], rs[:], asked, rooted)
                sc.wait_ge(ready, 1)
                for c in range(CT):
                    nc.scalar.activation(out[:, c], acc[:, c], ACT.Silu, scale=col("conv_ln_g_2")[:, c:c + 1],
                                         bias=col("conv_ln_b_2")[:, c:c + 1])

            @block.vector
            def _(ve):
                step = Steps(ve, dve)
                step(nc.vector.memset(uT[:, :, 0:PAD], 0.0))
                ve.wait_ge(sig, 1)
                nc.vector.tensor_tensor(a[:], a[:], g[:], ALU.mult).then_inc(glu, 1)
                ve.wait_ge(turned, 1)
                step(nc.vector.tensor_copy(tapT[:].rearrange("p c k -> p (c k)"), bank[:, 3, 0:CT * CK]))
                ve.wait_ge(left, CT // 2)
                for j in range(CK):
                    for c in range(CT):
                        x, w = uT[:, c, j:j + S], tapT[:, c, j:j + 1]
                        if j == 0:
                            ins = nc.vector.tensor_scalar(acc[:, c], x, w, col("conv_b_2")[:, c:c + 1], ALU.mult, ALU.add)
                        else:
                            ins = nc.vector.scalar_tensor_tensor(acc[:, c], x, w, acc[:, c], ALU.mult, ALU.add)
                    step(ins)
                ve.sem_inc(centred, 1)
                ve.wait_ge(summed, 1)
                step(nc.vector.tensor_scalar(mean[:], bank[:, 4, 0:S], 1.0 / CW, None, ALU.mult))
                step(nc.vector.tensor_tensor(acc[:], acc[:], over(mean[:], 1, CT), ALU.subtract))
                step(nc.vector.tensor_tensor(sq[:], acc[:], acc[:], ALU.mult))
                ve.sem_inc(centred, 1)
                ve.wait_ge(summed, 2)
                step(nc.vector.tensor_scalar(var[:], bank[:, 5, 0:S], 1.0 / CW, 1e-6, ALU.mult, ALU.add))
                inverse_root(nc, step, var[:], rs[:], nt[:], asked, rooted)
                step(nc.vector.tensor_tensor(acc[:], acc[:], over(rs[:], 1, CT), ALU.mult))
                ve.sem_inc(ready, 1)


def merge(chip, hT, yT, weights, next_weights):
    nc, ring, d, bank = chip.nc, chip.ring, chip.dram, chip.psum
    body, rounds = 16, D // NB
    span = ((0, GH, 6), (GH, GH + 2, 0), (GH + 2, KT, 2))
    with Stage(chip, "mg") as st:
        split = Split(st, ring, hT, body, plain=KC)
        merged = hT[:].rearrange("p (t k) s -> p t (k s)", t=T)
        gate = st.sb("gate", [P, 3, T, NB])
        brow = st.sb("brow", [1, 3, NB])
        biases = d["b_gate_2"].rearrange("a (b n) -> a b n", b=3)
        b_in, sig, used, taken, dve, turned, left, left2 = (
            st.sem(n) for n in ("b_in", "sig", "used", "taken", "dve", "turned", "left", "left2"))
        with nc.Block() as block:
            @block.sync
            def _(sp):
                ring.rest(sp, weights, rounds, body)
                ring.first(sp, next_weights)

            @block.tensor
            def _(pe):
                split.begin_tensor(pe)
                with pe.Fori(0, rounds) as i:
                    pe.wait_ge(b_in, i * 16 + 16)
                    pe.wait_ge(used, i * 3 + 3)
                    for b in range(3):
                        for t in range(T):
                            nc.tensor.matmul(bank[:, 2 * b + t], chip.c("ones")[0:1, :], brow[0:1, b],
                                             start=True, stop=False)
                        for c in range(KC):
                            split.use(pe, b * KC + c, i, lambda t, b=b: bank[:, 2 * b + t], split.parts,
                                      c * KC, False, c == KC - 1)
                    for c in range(KC):
                        def work(w, c=c):
                            for k in range(KC):
                                n = c * KC + k
                                lo, hi, pair = next(s for s in span if s[0] <= n < s[1])
                                for t in range(T):
                                    mm = nc.tensor.matmul(bank[:, pair + t], yT[:, n, t * P:(t + 1) * P], w[:, k],
                                                          start=(n == lo), stop=(n == hi - 1))
                            return mm
                        if c == 2:
                            pe.wait_ge(sig, i * 3 + 2)
                        ring.use(pe, 3 * KC + c, i, body, work)
                for g in range(KT // 2):
                    if g == 0:
                        pe.wait_ge(taken, rounds + 1)
                    if g >= 4:
                        pe.wait_ge((left, left2)[g % 2], g // 2 - 1)
                    turn(nc, pe, bank[:, g % 4], chip.c("ident"),
                         [merged[:, t, k * P:(k + 1) * P] for k in (2 * g, 2 * g + 1) for t in range(T)], turned)

            @block.scalar
            def _(sc):
                sc.dma_start(brow[:], biases[:, :, 0:NB]).then_inc(b_in, 16)
                split.begin_scalar(sc)

                def round_(i, last):
                    for b in range(3):
                        if b < 2:
                            split.chunks(split.hi, sc, i, b * KC + 2, b * KC + KC + 2)
                        else:
                            split.chunks(split.hi, sc, i, 2 * KC + 2, 3 * KC)
                            if not last:
                                split.chunks(split.hi, sc, i, body, body + 2)
                        if b == 0:
                            sc.wait_ge(taken, i + 1)
                        ring.done(sc, b * KC + KC - 1, i, body)
                        nc.scalar.activation(gate[:, b], bank[:, 2 * b:2 * b + 2], ACT.Sigmoid).then_inc(sig, 1)
                    if not last:
                        sc.dma_start(brow[:], biases[:, :, bass.ds(i * NB + NB, NB)]).then_inc(b_in, 16)

                with sc.Fori(0, rounds - 1) as i:
                    round_(i, False)
                round_(rounds - 1, True)
                for g in range(0, KT // 2, 2):
                    sc.wait_ge(turned, g + 1)
                    nc.scalar.copy(yT[:, 2 * g:2 * g + 2], bank[:, g % 4].rearrange("p (k s) -> p k s", k=2)).then_inc(left, 1)

            @block.vector
            def _(ve):
                ve.sem_inc(used, 3)
                ve.sem_inc(taken, 1)
                split.begin_vector(ve)

                def round_(i, last):
                    split.chunks(split.lo, ve, i, 2, 3 * KC)
                    if not last:
                        split.chunks(split.lo, ve, i, body, body + 2)
                    ve.wait_ge(sig, i * 3 + 3)
                    for b, (_, end, pair) in enumerate(span):
                        ring.done(ve, 3 * KC + (end - 1) // KC, i, body)
                        nc.vector.tensor_tensor(gate[:, b], gate[:, b], bank[:, pair:pair + 2], ALU.mult).then_inc(used, 1)
                    ve.wait_ge(used, i * 3 + 6)
                    nc.vector.tensor_tensor(gate[:, 0], gate[:, 0], gate[:, 1], ALU.add).then_inc(dve, 1)
                    ve.wait_ge(dve, i + 1)
                    cols = slice(i * NB, i * NB + NB) if isinstance(i, int) else bass.ds(i * NB, NB)
                    nc.vector.tensor_tensor(merged[:, :, cols], gate[:, 0], gate[:, 2], ALU.add).then_inc(taken, 1)

                with ve.Fori(0, rounds - 1) as i:
                    round_(i, False)
                round_(rounds - 1, True)
                for g in range(1, KT // 2, 2):
                    ve.wait_ge(turned, g + 1)
                    nc.vector.tensor_copy(yT[:, 2 * g:2 * g + 2], bank[:, g % 4].rearrange("p (k s) -> p k s", k=2)).then_inc(left2, 1)
        ring.used(rounds, body)


def output_product(chip, act, out, weights, next_weights):
    with Stage(chip, "wo") as st:
        square_product(chip, st, act, weights, next_weights, lambda sp: None, lambda ve: None,
                       lambda n, pair: chip.nc.vector.tensor_copy(out[:, :, n], pair))


def residual(chip, name, x, y, part, post):
    nc, d = chip.nc, chip.dram
    with Stage(chip, name) as st:
        gate, lo, bias, weight = (st.sb(n, [P, D]) for n in ("gate", "lo", "bias", "weight"))
        junk = st.sb("junk", [P, D])
        ss, rs, nt = (st.sb(n, [P, T]) for n in ("ss", "rs", "nt"))
        loaded, dve, summed, asked, rooted = (st.sem(n) for n in ("loaded", "dve", "summed", "asked", "rooted"))
        with nc.Block() as block:
            @block.sync
            def _(sp):
                at = slice(part * D, (part + 1) * D)
                sp.dma_start(gate[:], row(d["mod"][0:1, at])).then_inc(loaded, 16)
                sp.dma_start(lo[:], row(d["mod"][1:2, at])).then_inc(loaded, 16)
                sp.dma_start(bias[:], row(d["b_ada_2"][:, at])).then_inc(loaded, 16)
                sp.dma_start(weight[:], row(d[post])).then_inc(loaded, 16)

            @block.scalar
            def _(sc):
                for t in range(T):
                    nc.scalar.activation(junk[:], y[:, t], ACT.Square, accum_out=ss[:, t:t + 1]).then_inc(summed, 1)
                    sc.wait_ge(summed, t + 1)
                root(nc, ss[:], rs[:], asked, rooted)

            @block.vector
            def _(ve):
                step = Steps(ve, dve)
                ve.wait_ge(loaded, 64)
                step(nc.vector.tensor_tensor(gate[:], gate[:], lo[:], ALU.add))
                step(nc.vector.tensor_tensor(gate[:], gate[:], bias[:], ALU.add))
                step(nc.vector.tensor_tensor(gate[:], gate[:], weight[:], ALU.mult))
                ve.wait_ge(summed, T)
                step(nc.vector.tensor_scalar(ss[:], ss[:], 1.0 / D, 1e-6, ALU.mult, ALU.add))
                inverse_root(nc, step, ss[:], rs[:], nt[:], asked, rooted)
                for t in range(T):
                    step(nc.vector.scalar_tensor_tensor(y[:, t], y[:, t], rs[:, t:t + 1], gate[:], ALU.mult, ALU.mult))
                    step(nc.vector.tensor_tensor(x[:, t], x[:, t], y[:, t], ALU.add))


def load_order(d):
    ada = weight_blocks(d["w_ada_2"][0], NB)
    win, wout = weight_blocks(d["w_in"][0], W1), weight_blocks(d["w_out"][0], NB)
    gate = d["w_e_gate"][0].rearrange("e (c k p) n -> e c p k n", p=P, k=KC)
    up = d["w_e_up"][0].rearrange("e (c k p) n -> e c p k n", p=P, k=KC)
    down = d["w_e_down"][0].rearrange("e (k p) (b n) -> e b p k n", p=P, n=NB)

    def staggered(i, j, n_up, per):
        one = n_up + KC
        m, q = i * per + (j - n_up) // one, (j - n_up) % one
        if isinstance(i, int) and m < 0:
            return True, 0, j
        if isinstance(i, int) and m == SLICES - 1:
            return False, m, q
        return (True, m + 1, q) if q < n_up else (False, m, q - n_up)

    def expert(i, j):
        is_up, e, q = staggered(i, j, 8, 2)
        return chunk_of((gate, up)[q // 4] if is_up else down, e, q % 4)

    win2, w_gate = weight_blocks(d["w_in_2"][0], W2), weight_blocks(d["w_gate_2"][0], NB)
    w_abc, w_o = weight_blocks(d["w_abc"], NB), weight_blocks(d["w_o_2"][0], NB)
    w_up = weight_blocks(d["w_up_2"][0], NB)
    w_down = d["w_down_2"][0].rearrange("(f k p) (b n) -> f b p k n", p=P, k=KC, n=NB)

    def merged(i, j):
        if j >= 3 * KC:
            return chunk_of(w_abc, i, j - 3 * KC)
        return chunk_of(w_gate, i + (j // KC) * (D // NB), j % KC)

    def mlp(i, j):
        is_up, f, q = staggered(i, j, 4, 2)
        return chunk_of(w_up if is_up else w_down, f, q)

    return {
        "win": lambda i, j: chunk_of((win, ada)[j % 2], i * 2 + j // (2 * KC), j // 2 % KC),
        "wout": lambda i, j: chunk_of(wout, j // KC, j % KC),
        "moe": expert,
        "win2": lambda i, j: chunk_of(win2, i * 2 + j // KC, j % KC),
        "merge": merged,
        "wo": lambda i, j: chunk_of(w_o, j // KC, j % KC),
        "mlp": mlp,
    }


def program(nc, d):
    src = load_order(d)
    with ExitStack() as ctx:
        chip = Chip(nc, ctx, d)
        load_parameters(chip, src["win"])
        gain = lambda n: chip.cols[:, CC[n][0]:CC[n][0] + KT]
        actT = ctx.enter_context(nc.sbuf_tensor("actT", [P, KT, S], F32))
        comb = ctx.enter_context(nc.sbuf_tensor("comb", [P, T, NE], F32))
        with Stage(chip, "load_x") as st:
            x0, x0_in = st.sb("x", [P, T, D]), st.sem("x_in")
            with nc.Block() as block:
                @block.sync
                def _(sp):
                    sp.dma_start(x0[:], d["x"][0].rearrange("(t p) n -> p t n", p=P)).then_inc(x0_in, 16)
                    sp.wait_ge(x0_in, 16)
            normed(chip, "norm_mix", x0, actT, gain("g_mix"))
        project(chip, "proj1", actT, src["win"], W1, d["proj1"], 1, src["wout"], True)
        sparse_attention(chip, actT)
        rwkv(chip, actT)
        x1 = ctx.enter_context(nc.sbuf_tensor("x1", [P, T, D], F32))
        h2T = ctx.enter_context(nc.sbuf_tensor("h2T", [P, KT, S], F32))
        output_and_route(chip, actT, x1, h2T, comb, src["wout"], src["moe"])
        feed_forward(chip, h2T, x1, src["moe"], src["win2"], 2, True, comb)

        with nc.sbuf_tensor("modc", [P, 6 * KT], F32) as modc:
            part = lambda j: modc[:, j * KT:(j + 1) * KT]
            modulation_columns(chip, modc)
            normed(chip, "norm_mix2", x1, h2T, part(1), part(0))
            project(chip, "proj2", h2T, src["win2"], W2, d["proj2"], 0, src["merge"])
            hgrn(chip, actT)
            dilated_attention(chip, actT)
            convolution(chip, actT)
            y1 = h2T[:].rearrange("p (t k) s -> p t (k s)", t=T)
            merge(chip, h2T, actT, src["merge"], src["wo"])
            output_product(chip, actT, y1, src["wo"], src["mlp"])
            residual(chip, "res1", x1, y1, 2, "mix_norm_post_2")
            normed(chip, "norm_mlp", x1, h2T, part(4), part(3))
            y2 = actT[:].rearrange("p (t k) s -> p t (k s)", t=T)
            with nc.Block() as block:
                @block.vector
                def _(ve):
                    nc.vector.memset(y2, 0.0)
            feed_forward(chip, h2T, y2, src["mlp"], None, 2, False)
            residual(chip, "res2", x1, y2, 5, "mlp_norm_post_2")
        with Stage(chip, "store_x") as st:
            stored = st.sem("stored")
            with nc.Block() as block:
                @block.sync
                def _(sp):
                    sp.dma_start(d["out"][0].rearrange("(t p) n -> p t n", p=P), x1[:]).then_inc(stored, 16)
                    sp.wait_ge(stored, 16)


_INS = ["x", "g_mix", "w_in", "rwkv_shift_mix", "q_gain", "k_gain", "w0", "w_decay_up", "a0", "w_aicl_up",
        "w_gate_lora_up", "k_k", "k_a", "r_k", "ln_x_w", "ln_x_b", "w_out", "g_ffn", "w_route_group",
        "b_route_group", "w_route_expert", "b_route_expert", "w_e_gate", "w_e_up", "w_e_down", "c_2",
        "rel_bias_2", "hgrn_lb_logits_2", "w_ada_2", "b_ada_2", "mix_norm_pre_2", "mix_norm_post_2", "w_in_2",
        "w_gate_2", "b_gate_2", "hgrn_norm_w_2", "conv_w_2", "conv_b_2", "conv_ln_g_2", "conv_ln_b_2",
        "w_a_out_2", "w_b_out_2", "w_c_out_2", "w_o_2", "mlp_norm_pre_2", "mlp_norm_post_2", "w_up_2",
        "w_down_2"]


def declare(nc, arrays):
    d = {n: nc.dram_tensor(f"in_{n}", a.shape, F32, kind="ExternalInput").ap() for n, a in arrays.items()}
    d["out"] = nc.dram_tensor("out_x", (1, S, D), F32, kind="ExternalOutput").ap()
    d["mod"] = nc.dram_tensor("mod", (2, 6 * D), F32, kind="Internal").ap()
    d["proj1"] = nc.dram_tensor("proj1", (S + 1, IN1), F32, kind="Internal").ap()
    d["proj2"] = nc.dram_tensor("proj2", (S, IN2), F32, kind="Internal").ap()
    d["bias_rows"] = nc.dram_tensor("bias_rows", (BH, P, BVEC), F32, kind="Internal").ap()
    return d


def shape_tables():
    return {
        "consts": np.concatenate([CONSTS[k] for k in COL], axis=1),
        "rope_head": rotary(HD),
        "rope_idx": rotary(ID),
        "buckets": bucket_table(),
    }


def kernel(**inputs):
    import concourse.bacc as _bacc
    from concourse.bass_utils import run_bass_kernel_spmd as _run

    nc = _bacc.Bacc("TRN2", target_bir_lowering=False, num_devices=1)
    arrays = {n: np.ascontiguousarray(inputs[n]) for n in _INS}
    arrays["w_abc"] = np.concatenate([arrays.pop(n)[0] for n in ("w_a_out_2", "w_b_out_2", "w_c_out_2")], axis=0)
    arrays.update(shape_tables())
    program(nc, declare(nc, arrays))
    r = _run(nc, [{f"in_{n}": a for n, a in arrays.items()}], core_ids=[0])
    return r.results[0]["out_x"]
```
